# Optimizing a Trainium2 kernel written in Bass

```python
import math
import jax, jax.numpy as jnp
from jax import lax
import numpy as np

D_MODEL = 1024
BATCH = 1
SEQ = 256
DEPTH = 1

ATTN_HEADS = 8
HEAD_DIM = 64
ATTN_W = ATTN_HEADS * HEAD_DIM
MOBA_BLOCK = 256
MOBA_TOPK = 3
Q_CHUNK = 64
POOL_GROUPS = 4
POOL_GROUP_W = 128
POOL_W = POOL_GROUPS * POOL_GROUP_W
POOL_WINDOWS = (2, 4, 8, 16)
NUM_BUCKETS = 32
MAX_DISTANCE = 128
D_FF = 2816
CONV_W = 3
EPS = 1e-6
IN_W = 3 * ATTN_W + POOL_W + 2 * D_MODEL


def rms_norm(x, gain):
    xf = x.astype(jnp.float32)
    y = xf * lax.rsqrt(jnp.mean(xf * xf, axis=-1, keepdims=True) + EPS)
    return (y * gain.astype(jnp.float32)).astype(x.dtype)

def t5_bucket(dist):
    max_exact = NUM_BUCKETS // 2
    n = jnp.maximum(dist, 0)
    nf = jnp.maximum(n, 1).astype(jnp.float32)
    large = max_exact + (jnp.log(nf / max_exact) / math.log(MAX_DISTANCE / max_exact)
                         * (NUM_BUCKETS - max_exact)).astype(jnp.int32)
    large = jnp.minimum(large, NUM_BUCKETS - 1)
    return jnp.where(n < max_exact, n, large)

def moba_attention(q, k, v, rel_bias):
    B, H, S, Dh = q.shape
    n_blocks = -(-S // MOBA_BLOCK)
    s_pad = n_blocks * MOBA_BLOCK
    pad = ((0, 0), (0, 0), (0, s_pad - S), (0, 0))
    q = jnp.pad(q, pad)
    k = jnp.pad(k, pad)
    v = jnp.pad(v, pad)
    k_blocks = k.reshape(B, H, n_blocks, MOBA_BLOCK, Dh)
    v_blocks = v.reshape(B, H, n_blocks, MOBA_BLOCK, Dh)
    k_mean = jnp.mean(k_blocks.astype(jnp.float32), axis=3).astype(k.dtype)

    pos = jnp.arange(s_pad)
    q_blk = pos // MOBA_BLOCK
    gate = jnp.einsum('bhsd,bhnd->bhsn', q, k_mean).astype(jnp.float32)
    past = jnp.arange(n_blocks)[None, :] < q_blk[:, None]
    gate = jnp.where(past[None, None], gate, -jnp.inf)
    k_sel = min(MOBA_TOPK, n_blocks)
    _, sel = lax.top_k(gate, k_sel)
    sel_valid = jnp.arange(k_sel)[None, :] < q_blk[:, None]

    n_chunks = s_pad // Q_CHUNK
    q_c = q.reshape(B, H, n_chunks, Q_CHUNK, Dh).transpose(2, 0, 1, 3, 4)
    sel_c = sel.reshape(B, H, n_chunks, Q_CHUNK, k_sel).transpose(2, 0, 1, 3, 4)
    valid_c = sel_valid.reshape(n_chunks, Q_CHUNK, k_sel)
    bias_t = rel_bias.T.astype(jnp.float32)
    b_idx = jnp.arange(B)[:, None, None, None]
    h_idx = jnp.arange(H)[None, :, None, None]
    offs = jnp.arange(MOBA_BLOCK)
    scale = HEAD_DIM ** -0.5
    n_sel = k_sel * MOBA_BLOCK

    def chunk_fn(args):
        ci, qc, selc, validc = args
        qpos = ci * Q_CHUNK + jnp.arange(Q_CHUNK)
        own = (ci * Q_CHUNK) // MOBA_BLOCK
        k_own = lax.dynamic_index_in_dim(k_blocks, own, axis=2, keepdims=False)
        v_own = lax.dynamic_index_in_dim(v_blocks, own, axis=2, keepdims=False)
        dist_own = qpos[:, None] - (own * MOBA_BLOCK + offs)[None, :]
        bias_own = bias_t[:, t5_bucket(dist_own)]
        logit_own = jnp.einsum('bhqd,bhkd->bhqk', qc, k_own).astype(jnp.float32) * scale + bias_own
        logit_own = jnp.where(dist_own >= 0, logit_own, -jnp.inf)
        k_g = k_blocks[b_idx, h_idx, selc]
        v_g = v_blocks[b_idx, h_idx, selc]
        kpos_sel = selc[..., None] * MOBA_BLOCK + offs
        dist_sel = qpos[None, None, :, None, None] - kpos_sel
        bias_sel = bias_t[h_idx[..., None], t5_bucket(dist_sel)]
        logit_sel = jnp.einsum('bhqd,bhqnkd->bhqnk', qc, k_g).astype(jnp.float32) * scale + bias_sel
        logit_sel = jnp.where(validc[None, None, :, :, None], logit_sel, -jnp.inf)
        logits = jnp.concatenate([logit_sel.reshape(B, H, Q_CHUNK, n_sel), logit_own], axis=-1)
        prob = jax.nn.softmax(logits, axis=-1)
        p_sel = prob[..., :n_sel].reshape(B, H, Q_CHUNK, k_sel, MOBA_BLOCK).astype(v.dtype)
        p_own = prob[..., n_sel:].astype(v.dtype)
        return (jnp.einsum('bhqnk,bhqnkd->bhqd', p_sel, v_g)
                + jnp.einsum('bhqk,bhkd->bhqd', p_own, v_own))

    out = lax.map(chunk_fn, (jnp.arange(n_chunks), q_c, sel_c, valid_c))
    out = out.transpose(1, 2, 0, 3, 4).reshape(B, H, s_pad, Dh)
    return out[:, :, :S]

def multiscale_pool(p):
    B, S, G, Cg = p.shape
    pf = p.astype(jnp.float32)
    cs = jnp.concatenate([jnp.zeros((B, 1, G, Cg), jnp.float32), jnp.cumsum(pf, axis=1)], axis=1)
    win = jnp.array(POOL_WINDOWS, jnp.int32)
    t = jnp.arange(S)
    lo = jnp.maximum(t[:, None] + 1 - win[None, :], 0)
    cs_lo = cs[:, lo, jnp.arange(G)[None, :], :]
    count = jnp.minimum(t[:, None] + 1, win[None, :]).astype(jnp.float32)
    mean = (cs[:, 1:] - cs_lo) / count[None, :, :, None]
    return (mean - pf).astype(p.dtype)

def causal_dwconv(u, w, b):
    C = u.shape[-1]
    y = lax.conv_general_dilated(u, w[:, None, :].astype(u.dtype), window_strides=(1,),
                                 padding=((CONV_W - 1, 0),),
                                 dimension_numbers=('NWC', 'WIO', 'NWC'),
                                 feature_group_count=C)
    return y + b

def first_inputs(seed: int = 0) -> dict:
    key = jax.random.key(seed)
    ks = jax.random.split(key, 20)
    L, D = DEPTH, D_MODEL
    nrm = lambda k, shape, s: jax.random.normal(k, shape, jnp.float32) * s
    return {
        "x": nrm(ks[0], (BATCH, SEQ, D), 1.0),
        "c": nrm(ks[1], (BATCH, D), 1.0),
        "ada_w": nrm(ks[2], (L, D, 6 * D), 0.1 * D ** -0.5),
        "ada_b": nrm(ks[3], (L, 6 * D), 0.02),
        "norm1_g": 1.0 + nrm(ks[4], (L, D), 0.05),
        "w_in": nrm(ks[5], (L, D, IN_W), D ** -0.5),
        "q_norm_g": 1.0 + nrm(ks[6], (L, HEAD_DIM), 0.05),
        "k_norm_g": 1.0 + nrm(ks[7], (L, HEAD_DIM), 0.05),
        "rel_bias": nrm(ks[8], (NUM_BUCKETS, ATTN_HEADS), 0.5),
        "pool_w": nrm(ks[9], (L, POOL_GROUPS, POOL_GROUP_W, POOL_GROUP_W), POOL_GROUP_W ** -0.5),
        "pool_scale": 1.0 + nrm(ks[10], (L, POOL_W), 0.1),
        "w_branch_attn": nrm(ks[11], (L, ATTN_W, D), ATTN_W ** -0.5),
        "w_branch_pool": nrm(ks[12], (L, POOL_W, D), POOL_W ** -0.5),
        "w_out": nrm(ks[13], (L, D, D), D ** -0.5),
        "norm2_g": 1.0 + nrm(ks[14], (L, D), 0.05),
        "w_up": nrm(ks[15], (L, D, 2 * D_FF), D ** -0.5),
        "conv_w": nrm(ks[16], (L, CONV_W, 2 * D_FF), CONV_W ** -0.5),
        "conv_b": nrm(ks[17], (L, 2 * D_FF), 0.02),
        "w_down": nrm(ks[18], (L, D_FF, D), D_FF ** -0.5),
    }

def first_block(x, c, ada_w, ada_b, norm1_g, w_in, q_norm_g, k_norm_g, rel_bias, pool_w,
              pool_scale, w_branch_attn, w_branch_pool, w_out, norm2_g, w_up, conv_w, conv_b,
              w_down):
    B, S, D = x.shape
    split_at = [ATTN_W, 2 * ATTN_W, 3 * ATTN_W, 3 * ATTN_W + POOL_W, 3 * ATTN_W + POOL_W + D_MODEL]
    c_act = jax.nn.silu(c)
    for l in range(DEPTH):
        mod = c_act @ ada_w[l] + ada_b[l]
        shift1, scale1, gate1, shift2, scale2, gate2 = [m[:, None, :] for m in jnp.split(mod, 6, axis=-1)]

        h = rms_norm(x, norm1_g[l]) * (1 + scale1) + shift1
        z = h @ w_in[l]
        q, k, v, p, g_attn, g_pool = jnp.split(z, split_at, axis=-1)
        heads = lambda t: t.reshape(B, S, ATTN_HEADS, HEAD_DIM).transpose(0, 2, 1, 3)
        q = rms_norm(heads(q), q_norm_g[l])
        k = rms_norm(heads(k), k_norm_g[l])
        attn = moba_attention(q, k, heads(v), rel_bias)
        attn = attn.transpose(0, 2, 1, 3).reshape(B, S, ATTN_W)
        pool = multiscale_pool(p.reshape(B, S, POOL_GROUPS, POOL_GROUP_W))
        pool = jnp.einsum('bsgc,gcd->bsgd', pool, pool_w[l]).reshape(B, S, POOL_W) * pool_scale[l]
        merged = (jax.nn.sigmoid(g_attn) * (attn @ w_branch_attn[l])
                  + jax.nn.sigmoid(g_pool) * (pool @ w_branch_pool[l]))
        x = x + gate1 * (merged @ w_out[l])

        h2 = rms_norm(x, norm2_g[l]) * (1 + scale2) + shift2
        u = causal_dwconv(h2 @ w_up[l], conv_w[l], conv_b[l])
        u_g, u_v = jnp.split(u, 2, axis=-1)
        x = x + gate2 * ((jax.nn.silu(u_g) * u_v) @ w_down[l])
    return x


DEPTH_2 = 2

N_MIXERS = 2
A_Q_HEADS = D_MODEL // HEAD_DIM
A_KV_HEADS = A_Q_HEADS // 4
A_GROUP = A_Q_HEADS // A_KV_HEADS
WINDOW = 128
B_HEADS = D_MODEL // HEAD_DIM
BLOCK = 128
REL_BUCKETS = 32
REL_MAX_DIST = 128
FORGET_BIAS_INIT = 2.0
N_A_LAYERS = (DEPTH_2 + 1) // 2
N_B_LAYERS = DEPTH_2 // 2
A_IN = (A_Q_HEADS + 2 * A_KV_HEADS) * HEAD_DIM
B_IN = 3 * B_HEADS * HEAD_DIM + B_HEADS


def rmsnorm(x, g):
    xf = x.astype(jnp.float32)
    y = xf * lax.rsqrt(jnp.mean(xf * xf, axis=-1, keepdims=True) + EPS) * g.astype(jnp.float32)
    return y.astype(x.dtype)

def modulate(x, g, shift, scale):
    return rmsnorm(x, g) * (1 + scale[:, None, :]) + shift[:, None, :]

def swiglu(h, w13, w2):
    gate, up = jnp.split(h @ w13, 2, axis=-1)
    return (jax.nn.silu(gate) * up) @ w2

def rel_bucket(dist):
    n = jnp.maximum(dist, 0)
    max_exact = REL_BUCKETS // 2
    nf = jnp.maximum(n, 1).astype(jnp.float32)
    large = max_exact + (jnp.log(nf / max_exact) / math.log(REL_MAX_DIST / max_exact)
                         * (REL_BUCKETS - max_exact)).astype(jnp.int32)
    large = jnp.minimum(large, REL_BUCKETS - 1)
    return jnp.where(n < max_exact, n, large)

def swa_mixer(h, w_in, w_out, q_g, k_g, sink, rel_bias):
    B, S, _ = h.shape
    nblk = S // BLOCK
    proj = h @ w_in
    q, k, v = jnp.split(proj, [A_Q_HEADS * HEAD_DIM, (A_Q_HEADS + A_KV_HEADS) * HEAD_DIM], axis=-1)
    q = rmsnorm(q.reshape(B, S, A_KV_HEADS, A_GROUP, HEAD_DIM), q_g) * (HEAD_DIM ** -0.5)
    k = rmsnorm(k.reshape(B, S, A_KV_HEADS, HEAD_DIM), k_g)
    v = v.reshape(B, S, A_KV_HEADS, HEAD_DIM)
    pad = ((0, 0), (BLOCK, 0), (0, 0), (0, 0))
    kp = jnp.pad(k, pad)
    vp = jnp.pad(v, pad)
    qi = jnp.arange(BLOCK)[:, None] + BLOCK
    kj = jnp.arange(2 * BLOCK)[None, :]
    dist = qi - kj
    band = (dist >= 0) & (dist < WINDOW)
    bias = jnp.transpose(rel_bias[rel_bucket(dist)], (2, 0, 1)).astype(jnp.float32)
    bias = bias.reshape(A_KV_HEADS, A_GROUP, BLOCK, 2 * BLOCK)
    sink_f = sink.astype(jnp.float32).reshape(A_KV_HEADS, A_GROUP)[None, :, :, None]

    def block(i):
        start = i * BLOCK
        qb = lax.dynamic_slice_in_dim(q, start, BLOCK, axis=1)
        kb = lax.dynamic_slice_in_dim(kp, start, 2 * BLOCK, axis=1)
        vb = lax.dynamic_slice_in_dim(vp, start, 2 * BLOCK, axis=1)
        s = jnp.einsum('bqhgd,bkhd->bhgqk', qb, kb).astype(jnp.float32) + bias
        valid = band & (start - BLOCK + kj >= 0)
        s = jnp.where(valid, s, -jnp.inf)
        m = jnp.maximum(jnp.max(s, axis=-1), sink_f)
        p = jnp.exp(s - m[..., None])
        denom = jnp.sum(p, axis=-1) + jnp.exp(sink_f - m)
        p = p / denom[..., None]
        return jnp.einsum('bhgqk,bkhd->bqhgd', p.astype(vb.dtype), vb)

    out = lax.map(block, jnp.arange(nblk))
    out = jnp.moveaxis(out, 0, 1).reshape(B, S, A_Q_HEADS * HEAD_DIM)
    return out @ w_out

def fox_mixer(h, w_in, w_out, b_f, q_g, k_g):
    B, S, _ = h.shape
    nblk = S // BLOCK
    HD = B_HEADS * HEAD_DIM
    proj = h @ w_in
    q, k, v, fl = jnp.split(proj, [HD, 2 * HD, 3 * HD], axis=-1)
    q = rmsnorm(q.reshape(B, S, B_HEADS, HEAD_DIM), q_g) * (HEAD_DIM ** -0.5)
    k = rmsnorm(k.reshape(B, S, B_HEADS, HEAD_DIM), k_g)
    v = v.reshape(B, S, B_HEADS, HEAD_DIM)
    log_f = jax.nn.log_sigmoid(fl.astype(jnp.float32) + b_f.astype(jnp.float32))
    F = jnp.transpose(jnp.cumsum(log_f, axis=1), (0, 2, 1))
    kpos = jnp.arange(S)

    def block(i):
        start = i * BLOCK
        qb = lax.dynamic_slice_in_dim(q, start, BLOCK, axis=1)
        Fq = lax.dynamic_slice_in_dim(F, start, BLOCK, axis=2)
        s = jnp.einsum('bqhd,bkhd->bhqk', qb, k).astype(jnp.float32)
        s = s + Fq[..., None] - F[:, :, None, :]
        qpos = start + jnp.arange(BLOCK)
        s = jnp.where(kpos[None, :] <= qpos[:, None], s, -jnp.inf)
        p = jax.nn.softmax(s, axis=-1)
        return jnp.einsum('bhqk,bkhd->bqhd', p.astype(v.dtype), v)

    out = lax.map(block, jnp.arange(nblk))
    out = jnp.moveaxis(out, 0, 1).reshape(B, S, HD)
    return out @ w_out

def second_inputs(seed: int = 0) -> dict:
    key = jax.random.key(seed)
    ks = jax.random.split(key, 20)
    D = D_MODEL

    def nrm(k, shape, s):
        return jax.random.normal(k, shape, jnp.float32) * s

    return {
        'x': nrm(ks[0], (BATCH, SEQ, D), 1.0),
        'c': nrm(ks[1], (BATCH, D), 1.0),
        'ada_w': nrm(ks[2], (DEPTH_2, D, 9 * D), 0.5 * D ** -0.5),
        'ada_b': nrm(ks[3], (DEPTH_2, 9 * D), 0.02),
        'norm_g': 1.0 + nrm(ks[4], (DEPTH_2, 3, D), 0.02),
        'ffn_w13': nrm(ks[5], (DEPTH_2, 2, D, 2 * D_FF), D ** -0.5),
        'ffn_w2': nrm(ks[6], (DEPTH_2, 2, D_FF, D), D_FF ** -0.5),
        'rel_bias': nrm(ks[7], (REL_BUCKETS, A_Q_HEADS), 0.5),
        'swa_w_in': nrm(ks[8], (N_A_LAYERS, D, A_IN), D ** -0.5),
        'swa_w_out': nrm(ks[9], (N_A_LAYERS, A_Q_HEADS * HEAD_DIM, D), (A_Q_HEADS * HEAD_DIM) ** -0.5),
        'swa_q_g': 1.0 + nrm(ks[10], (N_A_LAYERS, HEAD_DIM), 0.02),
        'swa_k_g': 1.0 + nrm(ks[11], (N_A_LAYERS, HEAD_DIM), 0.02),
        'swa_sink': nrm(ks[12], (N_A_LAYERS, A_Q_HEADS), 0.5),
        'fox_w_in': nrm(ks[13], (N_B_LAYERS, D, B_IN), D ** -0.5),
        'fox_w_out': nrm(ks[14], (N_B_LAYERS, B_HEADS * HEAD_DIM, D), (B_HEADS * HEAD_DIM) ** -0.5),
        'fox_b_f': FORGET_BIAS_INIT + nrm(ks[15], (N_B_LAYERS, B_HEADS), 0.1),
        'fox_q_g': 1.0 + nrm(ks[16], (N_B_LAYERS, HEAD_DIM), 0.02),
        'fox_k_g': 1.0 + nrm(ks[17], (N_B_LAYERS, HEAD_DIM), 0.02),
    }

def second_block(x, c, ada_w, ada_b, norm_g, ffn_w13, ffn_w2, rel_bias,
              swa_w_in, swa_w_out, swa_q_g, swa_k_g, swa_sink,
              fox_w_in, fox_w_out, fox_b_f, fox_q_g, fox_k_g):
    B = x.shape[0]
    c_act = jax.nn.silu(c)
    for layer in range(DEPTH_2):
        mod = (c_act @ ada_w[layer] + ada_b[layer]).reshape(B, 3, 3, D_MODEL)
        h = modulate(x, norm_g[layer, 0], mod[:, 0, 0], mod[:, 0, 1])
        x = x + 0.5 * mod[:, 0, 2][:, None, :] * swiglu(h, ffn_w13[layer, 0], ffn_w2[layer, 0])
        h = modulate(x, norm_g[layer, 1], mod[:, 1, 0], mod[:, 1, 1])
        j = layer // N_MIXERS
        if layer % N_MIXERS == 0:
            y = swa_mixer(h, swa_w_in[j], swa_w_out[j], swa_q_g[j], swa_k_g[j], swa_sink[j], rel_bias)
        else:
            y = fox_mixer(h, fox_w_in[j], fox_w_out[j], fox_b_f[j], fox_q_g[j], fox_k_g[j])
        x = x + mod[:, 1, 2][:, None, :] * y
        h = modulate(x, norm_g[layer, 2], mod[:, 2, 0], mod[:, 2, 1])
        x = x + 0.5 * mod[:, 2, 2][:, None, :] * swiglu(h, ffn_w13[layer, 1], ffn_w2[layer, 1])
    return x


def setup_inputs(seed=0):
    out = dict(first_inputs(seed))
    for name, value in second_inputs(seed + 1).items():
        if name != "x":
            out[name + "_2"] = value
    return out


def reference(
    x, c, ada_w, ada_b, norm1_g, w_in, q_norm_g, k_norm_g, rel_bias, pool_w, pool_scale,
    w_branch_attn, w_branch_pool, w_out, norm2_g, w_up, conv_w, conv_b, w_down, c_2, ada_w_2,
    ada_b_2, norm_g_2, ffn_w13_2, ffn_w2_2, rel_bias_2, swa_w_in_2, swa_w_out_2, swa_q_g_2,
    swa_k_g_2, swa_sink_2, fox_w_in_2, fox_w_out_2, fox_b_f_2, fox_q_g_2, fox_k_g_2,
):
    x = first_block(
        x, c, ada_w, ada_b, norm1_g, w_in, q_norm_g, k_norm_g, rel_bias, pool_w, pool_scale,
        w_branch_attn, w_branch_pool, w_out, norm2_g, w_up, conv_w, conv_b, w_down,
    )
    return second_block(
        x, c_2, ada_w_2, ada_b_2, norm_g_2, ffn_w13_2, ffn_w2_2, rel_bias_2, swa_w_in_2,
        swa_w_out_2, swa_q_g_2, swa_k_g_2, swa_sink_2, fox_w_in_2, fox_w_out_2, fox_b_f_2,
        fox_q_g_2, fox_k_g_2,
    )


_drawn_inputs = setup_inputs


def setup_inputs(seed=0):
    import zlib

    import numpy as np

    out = dict(_drawn_inputs(seed))
    spreads = {}
    factors = {'ada_b': 3.575,
     'norm1_g': 8.0,
     'q_norm_g': 8.0,
     'k_norm_g': 8.0,
     'rel_bias': 8.0,
     'pool_scale': 8.0,
     'w_branch_attn': 6.409,
     'norm2_g': 8.0,
     'conv_b': 8.0,
     'norm_g_2': 7.436,
     'swa_q_g_2': 8.0,
     'swa_k_g_2': 8.0,
     'swa_sink_2': 64.0,
     'fox_b_f_2': 28.769,
     'fox_q_g_2': 8.0,
     'fox_k_g_2': 8.0}
    for name, (base, spread) in spreads.items():
        noise = np.random.default_rng([zlib.crc32(name.encode()), seed]).standard_normal(out[name].shape)
        drawn = base * np.exp(spread * noise) if base else spread * noise
        out[name] = __import__('jax').numpy.asarray(drawn.astype(out[name].dtype))
    for name, factor in factors.items():
        out[name] = (out[name] * factor).astype(out[name].dtype)
    return out
```

```python
from contextlib import ExitStack

import numpy as np

import concourse.bass as bass
from concourse import mybir

F32 = mybir.dt.float32
F32R = mybir.dt.float32r
BF16 = mybir.dt.bfloat16
ALU = mybir.AluOpType
ACT = mybir.ActivationFunctionType

P = 128
D = 1024
T = 256
KD = D // P
FF = 2816
HD = 64
UNIT = 2048
CW = 256
NBUF = 3
PRO_PE = [0, 2]
PRO_DVE = [1, 3, 4, 5, 6, 7]
PRO = len(PRO_PE)
FIT = FF // CW
PAIRS = (FIT - 1) // 2
EPS = 1e-6
NEG = -1e30
LOWEST = -3e38

KINDS = ["moba", "conv", "ffn", "swa", "ffn", "ffn", "fox", "ffn"]
NUNITS = {"moba": 24, "conv": 3 * FIT, "ffn": 3 * FIT, "swa": 10, "fox": 16}
N_ADA = [16, 12, 12, 12, 12, 12, 12, 0]
W0 = [sum(NUNITS[k] for k in KINDS[:s]) for s in range(len(KINDS) + 1)]
A0 = [len(PRO_DVE) + sum(N_ADA[:s]) for s in range(len(KINDS) + 1)]
FFN_NO = [sum(k in ("conv", "ffn") for k in KINDS[:s]) for s in range(len(KINDS))]
HEADS = {"moba": 8, "swa": 16, "fox": 16}
HEAD0 = [sum(HEADS.get(k, 0) for k in KINDS[:s]) for s in range(len(KINDS))]
QK_UNITS = {"moba": [0, 1, 2, 3], "swa": [0, 2, 3, 4, 5], "fox": list(range(8))}
QK0 = [sum(len(QK_UNITS.get(k, [])) for k in KINDS[:s]) for s in range(len(KINDS))]
V_UNITS = {"moba": [4, 5], "swa": [1], "fox": [8, 9, 10, 11]}
V0 = [sum(len(V_UNITS.get(k, [])) for k in KINDS[:s]) for s in range(len(KINDS))]
OUT_UNITS = {"moba": 20, "swa": 6, "fox": 12}
ADA_AFTER = {
    "moba": [1, 2, 3, 4, 5, 6, 7, 8, 9, 10, 11, 12, 13, 14, 15, 20],
    "swa": [2, 3, 3, 4, 4, 5, 5, 6, 7, 8, 9, 10],
    "fox": [2, 3, 4, 5, 6, 7, 8, 9, 13, 14, 15, 16],
}

C_ADAB, C_N1, C_N2, C_NG2 = 0, 64, 72, 80
C_ADAB2, C_CONVB, C_PSCALE, C_GAIN = (128, 256), 200, 244, 248
C_CONVW = (328, 384, 428)

K_IDENT, K_HEADS, K_TRI, K_MASK, K_DUP, K_INV, K_END = 0, 128, 256, 384, 640, 896, 960
WINDOWS = (2, 4, 8, 16)
ROWS_LOADED = 23 * 16
SMALL_LOADED = 9 * 16


def at(base, i=None, per=0):
    return base if i is None else i * per + base


def build(nc, a, consts, buckets, out):
    ctx = ExitStack()
    with ctx:
        def sb(name, shape, dt=F32):
            return ctx.enter_context(nc.sbuf_tensor(name, shape, dt))

        def sem(name):
            return ctx.enter_context(nc.semaphore(name))

        raw = sb("raw", [P, NBUF, UNIT])
        hi = sb("hi", [P, NBUF, UNIT], F32R)
        lo = sb("lo", [P, NBUF, UNIT], F32R)
        ada = sb("ada", [P, 2, KD, CW])
        ada_sum = sb("ada_sum", [P, 2, CW])
        xT = sb("xT", [P, KD, T])
        h_hi = sb("h_hi", [P, KD, T], F32R)
        h_lo = sb("h_lo", [P, KD, T], F32R)
        QT = sb("QT", [P, 8, T])
        KT = sb("KT", [P, 8, T])
        V = sb("V", [P, 2, D])
        o_hi = sb("o_hi", [P, 8, T], F32R)
        o_lo = sb("o_lo", [P, 8, T], F32R)
        TB = sb("TB", [P, 16, T])
        sq = sb("sq", [P, 4, T])
        std = sb("std", [P, 2, 512])
        tn = sb("tn", [P, 4, T])
        work = sb("work", [P, 2048])
        cols = sb("cols", [P, 512])
        kon = sb("kon", [P, K_END])
        ones = sb("ones", [P, P])
        zeros = sb("zeros", [P, 512], BF16)
        pool_w = sb("pool_w", [P, 4, P])
        f_w = sb("f_w", [P, KD, 16])
        f_hi = sb("f_hi", [P, KD, 16], F32R)
        f_lo = sb("f_lo", [P, KD, 16], F32R)
        c_act = sb("c_act", [P, 16])
        modc = sb("modc", [P, 2, 24])
        acol = sb("acol", [P, 2, 8])
        gate0 = sb("gate0", [P, 8])
        eps = sb("eps", [P, 1])
        stat = sb("stat", [P, 3, 8])
        sink = sb("sink", [P, 16])
        c_rows = sb("c_rows", [16, P])
        warm = sb("warm", [P, 1])
        fb = sb("fb", [P, 2, 16])
        fz = sb("fz", [P, 5, 32])
        Fq = sb("Fq", [P, 2, 16])
        nFT = sb("nFT", [16, T])
        rel = sb("rel", [64, 24])

        banks = [ctx.enter_context(nc.psum_tensor(f"bank{b}", [P, 512], F32)) for b in range(8)]
        A, G, M, S = banks[0:4], banks[4:6], banks[6], banks[7]

        ident = kon[:, K_IDENT:K_IDENT + P]
        head_ones = kon[:, K_HEADS:K_HEADS + P]
        tri = kon[:, K_TRI:K_TRI + P]
        mask = kon[:, K_MASK:K_MASK + 2 * P]
        P_of = [work[:, 384 * n:384 * n + 384] for n in range(3)]
        PT_of = [work[:, 1152 + 384 * n:1536 + 384 * n] for n in range(2)]
        hid_hi = o_hi[:, 0:4, :].rearrange("p (a b) t -> p a b t", a=2)
        hid_lo = o_lo[:, 0:4, :].rearrange("p (a b) t -> p a b t", a=2)
        cv = QT[:, 0:4, :]
        sil = KT[:, 0:4, :].rearrange("p (a b) t -> p a b t", a=2)
        prod = KT[:, 4:6, :]
        rows = TB[:, 0:2, :].rearrange("p a (b c) -> p (a b) c", b=2)
        x_in = V
        tables = tn[0:33, 0:3, :].rearrange("p a b -> p (a b)")
        table_rows = V[0:16, 0, 0:768].rearrange("p (a b) -> p a b", a=2)

        scratch = nc.dram_tensor("bias_by_distance", (2, 16, 384), F32).ap()
        scratch_f = nc.dram_tensor("forget_rows", (16, T), F32).ap()

        raw_full = [sem(f"raw_full{n}") for n in range(NBUF)]
        ada_full = [sem(f"ada_full{n}") for n in range(2)]
        rows_full, small_full, x_full = sem("rows_full"), sem("small_full"), sem("x_full")
        c_full, c_turned = sem("c_full"), sem("c_turned")
        rows_clear = sem("rows_clear")
        bias_out, bias_in = sem("bias_out"), sem("bias_in")
        forget_out, stored = sem("forget_out"), sem("stored")
        ones_set, cols_done, c_done = sem("ones_set"), sem("cols_done"), sem("c_done")
        rows_turned, x_turned = sem("rows_turned"), sem("x_turned")
        bias_sum, bias_rows = sem("bias_sum"), sem("bias_rows")
        pro_done = sem("pro_done")
        f_hi_done, f_lo_done = sem("f_hi_done"), sem("f_lo_done")
        hi_ready, lo_ready, unit_done = sem("hi_ready"), sem("lo_ready"), sem("unit_done")
        ada_step, ada_ready, ada_used = sem("ada_step"), sem("ada_ready"), sem("ada_used")
        mod_ready = sem("mod_ready")
        x_ready, sq_ready, sq_used = sem("x_ready"), sem("sq_ready"), sem("sq_used")
        stats_done, std_ready, rstd_ready = sem("stats_done"), sem("std_ready"), sem("rstd_ready")
        t_ready, hhi_ready, h_ready = sem("t_ready"), sem("hhi_ready"), sem("h_ready")
        acc_zero, acc_done = sem("acc_zero"), sem("acc_done")
        cv_ready, tap_done, conv_done = sem("cv_ready"), sem("tap_done"), sem("conv_done")
        silu_ready, mul_done = sem("silu_ready"), sem("mul_done")
        hid_hi_done, hid_ready = sem("hid_hi_done"), sem("hid_ready")
        qsq_ready, qs_done, qstd_ready = sem("qsq_ready"), sem("qs_done"), sem("qstd_ready")
        qrs_ready, qk_ready, v_ready = sem("qrs_ready"), sem("qk_ready"), sem("v_ready")
        p_ready, sig_ready = sem("p_ready"), sem("sig_ready")
        dup_done, dup_ready = sem("dup_done"), sem("dup_ready")
        fl_done, fz_ready, f_exp, f_ln = sem("fl_done"), sem("fz_ready"), sem("f_exp"), sem("f_ln")
        lf_ready, cum_done, fq_ready = sem("lf_ready"), sem("cum_done"), sem("fq_ready")
        ft_done, nft_ready = sem("ft_done"), sem("nft_ready")
        qk_done, bias_ready, max_done = sem("qk_done"), sem("bias_ready"), sem("max_done")
        neg_done, am_done, exp_done = sem("neg_done"), sem("am_done"), sem("exp_done")
        den_ready, nm_done, tr_done = sem("den_ready"), sem("nm_done"), sem("tr_done")
        ptc_done, pv_done = sem("ptc_done"), sem("pv_done")
        ohi_done, olo_done = sem("ohi_done"), sem("olo_done")
        pool_step, pool_ready, pw_done = sem("pool_step"), sem("pool_ready"), sem("pw_done")
        ps_ready, phi_done, pool_split = sem("ps_ready"), sem("phi_done"), sem("pool_split")
        merge_a, merge_b, merge_s = sem("merge_a"), sem("merge_b"), sem("merge_s")
        merge_hi, merged = sem("merge_hi"), sem("merged")
        y_turned, y_ready = sem("y_turned"), sem("y_ready")

        def split_of(w):
            return w % NBUF

        def raw_of(w):
            return (w + PRO) % NBUF

        def all_rows(ap):
            return ap.rearrange("(k p) n -> p k n", p=P)


        ada_1 = all_rows(a["ada_w"][0])

        def ada_source(s, b):
            if s == 0:
                return ada_1[:, :, 2 * D + CW * b:2 * D + CW * (b + 1)]
            l, stage = divmod(s - 1, 3)
            first = 3 * D * stage
            src = all_rows(a["ada_w_2"][l])
            if isinstance(b, int):
                return src[:, :, first + CW * b:first + CW * (b + 1)]
            return src[:, :, bass.ds(b * CW + first, CW)]

        def unit_source(s, m):
            kind = KINDS[s]
            if kind == "moba":
                w_in = all_rows(a["w_in"][0])
                if m < 16:
                    return w_in[:, :, CW * m:CW * (m + 1)], KD
                if m < 20:
                    w = a["w_branch_attn"][0] if m % 2 == 0 else a["w_branch_pool"][0]
                    half = (m - 16) // 2
                    return all_rows(w)[:, :, 512 * half:512 * (half + 1)], 4
                return all_rows(a["w_out"][0])[:, :, CW * (m - 20):CW * (m - 19)], KD
            if kind == "swa":
                if m < 6:
                    c = [4, 5, 0, 1, 2, 3][m]
                    return all_rows(a["swa_w_in_2"][0])[:, :, CW * c:CW * (c + 1)], KD
                return all_rows(a["swa_w_out_2"][0])[:, :, CW * (m - 6):CW * (m - 5)], KD
            if m < 12:
                c = m // 2 + 4 * (m % 2) if m < 8 else m
                return all_rows(a["fox_w_in_2"][0])[:, :, CW * c:CW * (c + 1)], KD
            return all_rows(a["fox_w_out_2"][0])[:, :, CW * (m - 12):CW * (m - 11)], KD

        def ffn_weights(s):
            if KINDS[s] == "conv":
                return a["w_up"][0], a["w_down"][0]
            l, n = {2: (0, 0), 4: (0, 1), 5: (1, 0), 7: (1, 1)}[s]
            return a["ffn_w13_2"][l, n], a["ffn_w2_2"][l, n]

        block = ctx.enter_context(nc.Block())

        @block.sync
        def _(sp):
            def load(w, src, tiles, i=None):
                if w >= NBUF:
                    sp.wait_ge(lo_ready, at(w - NBUF + 1, i, 6))
                elif w + PRO >= NBUF:
                    sp.wait_ge(pro_done, w + PRO - NBUF + 1)
                dst = raw[:, raw_of(w), :].rearrange("p (k n) -> p k n", k=tiles)
                sp.dma_start(dst, src).then_inc(raw_full[raw_of(w)], 16)

            def load_ada(s, b, i=None):
                sp.wait_ge(ada_ready, at(A0[s] + b - 1, i, 2))
                n = b if i is None else i * 2 + b
                slot = (A0[s] + b) % 2
                sp.dma_start(ada[:, slot, :, :], ada_source(s, n)).then_inc(ada_full[slot], 16)

            sp.dma_start(ident, consts[:, K_IDENT:K_IDENT + P]).then_inc(c_full, 16)
            sp.dma_start(c_rows[0:8, :], a["c"][0].rearrange("(r c) -> r c", c=P)).then_inc(c_full, 16)
            sp.dma_start(c_rows[8:16, :], a["c_2"][0].rearrange("(r c) -> r c", c=P)).then_inc(c_full, 16)
            for r in range(8):
                if r == 2:
                    sp.dma_start(x_in[:, :, :], a["x"][0].rearrange("(t p) d -> p t d", p=P)).then_inc(x_full, 16)
                src = ada_1[:, :, CW * r:CW * (r + 1)]
                if r in PRO_PE:
                    n = PRO_PE.index(r)
                    dst = raw[:, n, :].rearrange("p (k n) -> p k n", k=KD)
                    sp.dma_start(dst, src).then_inc(raw_full[n], 16)
                else:
                    n = PRO_DVE.index(r)
                    if n >= 2:
                        sp.wait_ge(ada_ready, n - 1)
                    sp.dma_start(ada[:, n % 2, :, :], src).then_inc(ada_full[n % 2], 16)

            for s, kind in enumerate(KINDS):
                if kind in HEADS:
                    after = ADA_AFTER[kind]
                    b = 0
                    for m in range(NUNITS[kind]):
                        load(W0[s] + m, *unit_source(s, m))
                        while b < N_ADA[s] and (m >= 2 * b if b < 2 else after[b - 2] + NBUF <= m):
                            load_ada(s, b)
                            b += 1
                    late = list(range(b, N_ADA[s]))
                else:
                    up, down = ffn_weights(s)
                    up_v = all_rows(up)
                    down_v = down.rearrange("(k p) n -> p k n", p=P)
                    base = W0[s]
                    load(base, up_v[:, :, 0:CW], KD)
                    load(base + 1, up_v[:, :, FF:FF + CW], KD)
                    for b in late:
                        load_ada(s - 1, b)
                    for b in range(2 if N_ADA[s] else 0):
                        load_ada(s, b)
                    with sp.Fori(0, PAIRS) as i:
                        for e in range(2):
                            u = base + 2 + 3 * e
                            col = i * (2 * CW) + CW * (e + 1)
                            load(u, up_v[:, :, bass.ds(col, CW)], KD, i)
                            load(u + 1, up_v[:, :, bass.ds(col + FF, CW)], KD, i)
                            if N_ADA[s]:
                                load_ada(s, e + 2, i)
                            load(u + 2, down_v[:, bass.ds(i * 4 + 2 * e, 2), :], 2, i)
                    load(base + 3 * FIT - 1, down_v[:, 2 * FIT - 2:2 * FIT, :], 2)
                    late = []

            for t in range(2):
                sp.wait_ge(y_ready, 2 * (t + 1))
                sp.dma_start(out[0, P * t:P * (t + 1), :], V[:, t, :]).then_inc(stored, 16)
            sp.wait_ge(stored, 32)

        @block.gpsimd
        def _(pool):
            pool.dma_start(kon[:, P:K_END], consts[:, P:K_END]).then_inc(small_full, 16)
            pool.dma_start(tables, buckets).then_inc(small_full, 16)
            pool.wait_ge(ones_set, 1)
            pool.dma_start(rel[0:32, 0:8], a["rel_bias"]).then_inc(small_full, 16)
            pool.dma_start(rel[0:32, 8:24], a["rel_bias_2"]).then_inc(small_full, 16)
            pool.dma_start(f_w[:, :, :], all_rows(a["fox_w_in_2"][0])[:, :, 3 * D:3 * D + 16]).then_inc(small_full, 16)
            pool.dma_start(pool_w[:, :, :], a["pool_w"][0].rearrange("g c d -> c g d")).then_inc(small_full, 16)
            over_partitions = lambda ap: bass.AP(tensor=ap.tensor, offset=ap.offset, ap=[[0, P], [1, 16]])
            pool.dma_start(sink[:, :], over_partitions(a["swa_sink_2"][0:1, :])).then_inc(small_full, 16)
            for t in range(2):
                pool.dma_start(fb[:, t, :], over_partitions(a["fox_b_f_2"][0:1, :])).then_inc(small_full, 16)

            def by_distance(n, heads):
                src = bass.AP(tensor=scratch.tensor, offset=scratch.offset + n * 16 * 384,
                              ap=[[1, P], [384, heads], [1, T]])
                pool.dma_start(TB[:, 0:heads, :], src).then_inc(bias_in, 16)

            pool.wait_ge(bias_rows, 1)
            for n in range(2):
                heads = (8, 16)[n]
                pool.dma_start(scratch[n, 0:heads, :], table_rows[0:heads, n, :]).then_inc(bias_out, 16)
            pool.wait_ge(bias_out, 32)
            pool.wait_ge(cols_done, 2)
            by_distance(0, 8)
            pool.wait_ge(merged, 4)
            by_distance(1, 16)
            pool.wait_ge(nft_ready, 1)
            pool.dma_start(scratch_f[:, :], nFT[:, :]).then_inc(forget_out, 16)
            pool.wait_ge(forget_out, 16)
            src = bass.AP(tensor=scratch_f.tensor, offset=scratch_f.offset, ap=[[0, P], [1, 16 * T]])
            pool.dma_start(TB[:, :, :].rearrange("p a b -> p (a b)"), src).then_inc(bias_in, 16)

        @block.scalar
        def _(act):
            def split_hi(w, i=None):
                act.wait_ge(raw_full[raw_of(w)], at(16 * ((w + PRO) // NBUF + 1), i, 32))
                if w >= NBUF:
                    act.wait_ge(unit_done, at(w - NBUF + 1, i, 6))
                nc.scalar.activation(hi[:, split_of(w), :], raw[:, raw_of(w), :], ACT.Copy).then_inc(hi_ready, 1)

            next_hi = 0

            def split_through(s, u):
                nonlocal next_hi
                while next_hi <= W0[s] + u and next_hi < W0[-1]:
                    split_hi(next_hi)
                    next_hi += 1

            def norm_stats(s):
                nc.scalar.activation(warm[:, :], eps[:, :], ACT.Sqrt)
                for k in range(KD):
                    act.wait_ge(x_ready, KD * s + k + 1 + (k + 1) % 2 * (s == 0))
                    if k >= 4:
                        act.wait_ge(sq_used, (KD - 1) * s + k - 3)
                    nc.scalar.activation(sq[:, k % 4, :], xT[:, k, :], ACT.Square).then_inc(sq_ready, 1)
                act.wait_ge(stats_done, s + 1)
                nc.scalar.activation(std[:, 0, 0:T], S[:, 0:T], ACT.Sqrt, bias=eps[:, 0:1],
                                     scale=1.0 / D).then_inc(std_ready, 1)

            def norm_apply(s):
                for k in range(KD):
                    act.wait_ge(t_ready, KD * s + k + 1)
                    nc.scalar.activation(h_hi[:, k, :], tn[:, k % 4, :], ACT.Identity,
                                         bias=modc[:, s % 2, k:k + 1]).then_inc(hhi_ready, 1)

            def ffn_step(s, j, i=None):
                base, f = W0[s], FFN_NO[s]
                n = base + 3 * j
                gate, up = (n - 1, n) if j else (n, n + 1)
                if KINDS[s] == "conv":
                    def convolve_last(q):
                        tile = 2 * j + q % 2 + (FF // P) * (q // 2)
                        col = lambda c: cols[:, c + tile:c + tile + 1] if i is None else cols[:, bass.ds(i * 4 + c + tile, 1)]
                        nc.scalar.activation(cv[:, q, :], G[q // 2][:, T * (q % 2):T * (q % 2 + 1)], ACT.Identity,
                                             bias=col(C_CONVB), scale=col(C_CONVW[2])).then_inc(cv_ready, 1)

                    if j:
                        act.wait_ge(mul_done, at(j, i, 2))
                    act.wait_ge(unit_done, at(gate + 1, i, 6))
                    convolve_last(0)
                    convolve_last(1)
                    split_hi(n + 2, i)
                    act.wait_ge(conv_done, at(4 * j + 2, i, 8))
                    nc.scalar.activation(sil[:, j % 2, :, :], cv[:, 0:2, :], ACT.Silu).then_inc(silu_ready, 1)
                    act.wait_ge(unit_done, at(up + 1, i, 6))
                    convolve_last(2)
                    convolve_last(3)
                else:
                    split_hi(n + 2, i)
                    act.wait_ge(unit_done, at(gate + 1, i, 6))
                    nc.scalar.activation(sil[:, j % 2, :, :].rearrange("p a b -> p (a b)"), G[0][:, :],
                                         ACT.Silu).then_inc(silu_ready, 1)
                if n + 3 < W0[-1]:
                    split_hi(n + 3, i)
                    split_hi(n + 4, i)

            def q_square(s, u):
                q = QK_UNITS[KINDS[s]].index(u)
                act.wait_ge(unit_done, W0[s] + u + 1)
                if q >= 2:
                    act.wait_ge(qs_done, QK0[s] + q - 1)
                nc.scalar.activation(sq[:, 2 * (q % 2):2 * (q % 2) + 2, :].rearrange("p a b -> p (a b)"),
                                     G[u % 2][:, :], ACT.Square).then_inc(qsq_ready, 1)

            def q_std(s, q):
                act.wait_ge(qs_done, QK0[s] + q + 1)
                if q >= 2:
                    act.wait_ge(qk_ready, QK0[s] + q - 1)
                nc.scalar.activation(std[:, q % 2, :], S[:, :], ACT.Sqrt, bias=eps[:, 0:1],
                                     scale=1.0 / HD).then_inc(qstd_ready, 1)

            def v_copy(s, v):
                u = V_UNITS[KINDS[s]][v]
                act.wait_ge(unit_done, W0[s] + u + 1)
                if s == 0 and v == 0:
                    act.wait_ge(bias_out, 32)
                nc.scalar.activation(V[:, :, CW * v:CW * (v + 1)], G[u % 2][:, :].rearrange("p (a b) -> p a b", a=2),
                                     ACT.Copy).then_inc(v_ready, 1)

            def exps(s, h):
                n = HEAD0[s] + h
                st, pr = stat[:, n % 3, :], P_of[n % 3]
                act.wait_ge(am_done, n + 1)
                nc.scalar.activation(pr[:, 0:P], pr[:, 0:P], ACT.Exp, bias=st[:, 2:3], accum_out=st[:, 4:5])
                ins = nc.scalar.activation(pr[:, P:384], pr[:, P:384], ACT.Exp, bias=st[:, 3:4], accum_out=st[:, 5:6])
                if KINDS[s] == "swa":
                    ins = nc.scalar.activation(st[:, 6:8], st[:, 6:8], ACT.Exp)
                ins.then_inc(exp_done, 1)

            def pt_copy(s, h):
                n = HEAD0[s] + h
                act.wait_ge(tr_done, n + 1)
                if n >= 2:
                    act.wait_ge(pv_done, n - 1)
                dst = PT_of[n % 2].rearrange("p (a b) -> p a b", a=3)
                if KINDS[s] != "fox":
                    dst = dst[:, :, ::-1]
                nc.scalar.activation(dst, A[2][:, 0:384].rearrange("p (a b) -> p a b", a=3),
                                     ACT.Copy).then_inc(ptc_done, 1)

            def out_hi(s, pair):
                n = HEAD0[s] // 2 + pair
                act.wait_ge(pv_done, 2 * n + 2)
                nc.scalar.activation(o_hi[:, pair, :], (A[3], S)[n % 2][:, 0:T], ACT.Copy).then_inc(ohi_done, 1)

            def attention_step(s, t):
                nh = HEADS[KINDS[s]]
                if t < nh:
                    exps(s, t)
                if 0 <= t - 2 < nh:
                    pt_copy(s, t - 2)
                if 0 <= t - 4 < nh and (t - 4) % 2:
                    out_hi(s, (t - 4) // 2)

            act.wait_ge(c_turned, 1)
            nc.scalar.activation(c_act[:, :], S[:, 0:16], ACT.Silu).then_inc(c_done, 1)
            act.wait_ge(rows_clear, 1)
            r128 = lambda ap: ap.rearrange("(r c) -> r c", c=P)
            for tile, first, src in [
                (0, 0, r128(a["ada_b"][0])),
                (0, 64, r128(a["norm1_g"][0])), (0, 72, r128(a["norm2_g"][0])),
                (0, 80, a["norm_g_2"].rearrange("l s (r c) -> (l s r) c", c=P)),
                (1, 0, r128(a["ada_b_2"][0])), (1, 72, r128(a["conv_b"][0])), (1, 116, r128(a["pool_scale"][0])),
                (2, 0, r128(a["ada_b_2"][1])), (2, 72, r128(a["conv_w"][0, 0])),
                (3, 0, r128(a["conv_w"][0, 1])), (3, 44, r128(a["conv_w"][0, 2])),
            ]:
                act.dma_start(rows[first:first + src.shape[0], tile, :], src).then_inc(rows_full, 16)
            for n, name in enumerate(["q_norm_g", "k_norm_g", "swa_q_g_2", "swa_k_g_2", "fox_q_g_2", "fox_k_g_2"]):
                for c in range(2):
                    act.dma_start(rows[120 + n:121 + n, 1, HD * c:HD * (c + 1)], a[name][0:1, :]).then_inc(rows_full, 16)
            act.wait_ge(small_full, SMALL_LOADED)
            nc.scalar.activation(f_hi[:, :, :], f_w[:, :, :], ACT.Copy).then_inc(f_hi_done, 1)

            for s, kind in enumerate(KINDS):
                base = W0[s]
                norm_stats(s)
                split_through(0, 1)
                norm_apply(s)
                if kind in ("conv", "ffn"):
                    turns = PAIRS - (s == len(KINDS) - 1)
                    ffn_step(s, 0)
                    with act.Fori(0, turns) as i:
                        ffn_step(s, 1, i)
                        ffn_step(s, 2, i)
                    for j in range(1 + 2 * turns, FIT):
                        ffn_step(s, j)
                    next_hi = W0[s + 1] + 2
                elif kind == "moba":
                    for u in range(4):
                        split_through(s, u + 2)
                        q_square(s, u)
                        if u:
                            q_std(s, u - 1)
                    split_through(s, 6)
                    v_copy(s, 0)
                    q_std(s, 3)
                    for t in range(HEADS[kind] + 4):
                        attention_step(s, t)
                        if t == 2:
                            split_through(s, 7)
                            v_copy(s, 1)
                        if t in (4, 6):
                            split_through(s, 8 + (t - 4) // 2)
                            i = (t - 4) // 2
                            act.wait_ge(unit_done, base + 7 + i)
                            nc.scalar.activation(V[:, i, 512:1024], G[i % 2][:, :], ACT.Copy).then_inc(p_ready, 1)
                    for r in range(8):
                        split_through(s, 10 + r)
                        act.wait_ge(unit_done, base + 9 + r)
                        dst = (TB[:, 8 + 2 * r:10 + 2 * r, :] if r < 4 else
                               (QT if r < 6 else KT)[:, 4 + 2 * (r % 2):6 + 2 * (r % 2), :])
                        nc.scalar.activation(dst.rearrange("p a b -> p (a b)"), G[r % 2][:, :],
                                             ACT.Sigmoid).then_inc(sig_ready, 1)
                        if r == 5:
                            for g in range(4):
                                act.wait_ge(pw_done, g // 2 * 2 + 2)
                                nc.scalar.activation(sq[:, g, :], A[g // 2][:, T * (g % 2):T * (g % 2 + 1)], ACT.Copy,
                                                     scale=cols[:, C_PSCALE + g:C_PSCALE + g + 1]).then_inc(ps_ready, 1)
                    split_through(s, NUNITS[kind] + 1)
                elif kind == "swa":
                    split_through(s, 2)
                    q_square(s, 0)
                    split_through(s, 3)
                    q_std(s, 0)
                    v_copy(s, 0)
                    for u in range(2, 6):
                        split_through(s, u + 2)
                        if u == 2:
                            for n in range(2):
                                act.wait_ge(dup_done, n + 1)
                                nc.scalar.activation(KT[:, 4 + 2 * n:6 + 2 * n, :].rearrange("p a b -> p (a b)"),
                                                     A[n][:, :], ACT.Copy).then_inc(dup_ready, 1)
                        q_square(s, u)
                        if u > 2:
                            q_std(s, u - 2)
                    q_std(s, 4)
                    for t in range(HEADS[kind] + 4):
                        attention_step(s, t)
                        if t == 4:
                            split_through(s, 8)
                    split_through(s, NUNITS[kind] + 1)
                else:
                    for u in range(8):
                        split_through(s, u + 2)
                        q_square(s, u)
                        if u:
                            q_std(s, u - 1)
                        if u == 1:
                            act.wait_ge(fz_ready, 2)
                            nc.scalar.activation(fz[:, 2, :], fz[:, 1, :], ACT.Exp).then_inc(f_exp, 1)
                            act.wait_ge(f_exp, 1)
                            nc.scalar.activation(fz[:, 3, :], fz[:, 2, :], ACT.Ln, bias=ones[:, 0:1]).then_inc(f_ln, 1)
                    split_through(s, 10)
                    v_copy(s, 0)
                    q_std(s, 7)
                    for t in range(HEADS[kind] + 4):
                        attention_step(s, t)
                        if t in (3, 7, 11):
                            v = (t - 3) // 4 + 1
                            split_through(s, 10 + v)
                            v_copy(s, v)
                    split_through(s, NUNITS[kind] + 1)

        @block.vector
        def _(dve):
            pool_steps = 0

            def split_lo(w, i=None):
                dve.wait_ge(hi_ready, at(w + 1, i, 6))
                nc.vector.tensor_tensor(lo[:, split_of(w), :], raw[:, raw_of(w), :],
                                        hi[:, split_of(w), :].bitcast(F32), ALU.subtract).then_inc(lo_ready, 1)

            def ada_unit(s, b, i=None):
                ada_sum_of(A0[s] + b, 0 if s == 0 else 8, i)

            def ada_sum_of(n, c, i=None):
                slot = n % 2
                dve.wait_ge(ada_full[slot], at(16 * (n // 2 + 1), i, 16))
                if n >= 2:
                    dve.wait_ge(ada_used, at(n - 1, i, 2))
                acc = ada_sum[:, slot, :]
                nc.vector.tensor_scalar(acc, ada[:, slot, 0, :], c_act[:, c:c + 1], None, ALU.mult).then_inc(ada_step, 1)
                for k in range(1, KD):
                    dve.wait_ge(ada_step, at(7 * n + k, i, 14))
                    nc.vector.scalar_tensor_tensor(acc, in0=ada[:, slot, k, :], scalar=c_act[:, c + k:c + k + 1],
                                                   in1=acc, op0=ALU.mult, op1=ALU.add
                                                   ).then_inc(ada_step if k < KD - 1 else ada_ready, 1)

            next_lo = 0

            def split_through(s, u):
                nonlocal next_lo
                while next_lo <= W0[s] + u:
                    split_lo(next_lo)
                    for b, m in enumerate(ADA_AFTER[KINDS[s]]):
                        if m == next_lo - W0[s]:
                            ada_unit(s, b)
                    next_lo += 1

            def mod_columns(s):
                par = s % 2
                if s == 0:
                    dve.wait_ge(pro_done, PRO)
                    dve.wait_ge(ada_used, len(PRO_DVE))
                    nc.vector.tensor_tensor(modc[:, 0, 0:16], M[:, 0:16], cols[:, 0:16], ALU.add).then_inc(mod_ready, 1)
                    dve.wait_ge(mod_ready, 1)
                    gain = C_N1
                elif s == 1:
                    dve.wait_ge(ada_used, A0[1])
                    nc.vector.tensor_tensor(gate0[:, :], M[:, 0:8], cols[:, 16:24], ALU.add)
                    nc.vector.tensor_tensor(modc[:, 1, :], M[:, 8:32], cols[:, 24:48], ALU.add).then_inc(mod_ready, 1)
                    dve.wait_ge(mod_ready, 3)
                    gain = C_N2
                else:
                    l, stage = divmod(s - 2, 3)
                    first = C_ADAB2[l] + 24 * stage
                    dve.wait_ge(ada_used, A0[s])
                    nc.vector.tensor_tensor(modc[:, par, :], M[:, 0:24], cols[:, first:first + 24], ALU.add).then_inc(mod_ready, 1)
                    dve.wait_ge(mod_ready, 2 * s + 1)
                    gain = C_NG2 + 8 * (s - 2)
                if s >= 2 and KINDS[s] == "ffn":
                    nc.vector.tensor_scalar(modc[:, par, 16:24], modc[:, par, 16:24], 0.5, None, ALU.mult)
                nc.vector.scalar_tensor_tensor(acol[:, par, :], in0=modc[:, par, 8:16], scalar=1.0,
                                               in1=cols[:, gain:gain + 8], op0=ALU.add, op1=ALU.mult).then_inc(mod_ready, 1)
                dve.wait_ge(mod_ready, 2 * s + 2)

            def norm_stats(s):
                dve.wait_ge(std_ready, s + 1)
                nc.vector.reciprocal(std[:, 1, 0:T], std[:, 0, 0:T]).then_inc(rstd_ready, 1)
                dve.wait_ge(rstd_ready, s + 1)

            def norm_apply(s):
                par = s % 2
                for k in range(KD + 1):
                    if k < KD:
                        nc.vector.scalar_tensor_tensor(tn[:, k % 4, :], in0=xT[:, k, :], scalar=acol[:, par, k:k + 1],
                                                       in1=std[:, 1, 0:T], op0=ALU.mult, op1=ALU.mult).then_inc(t_ready, 1)
                    if k:
                        dve.wait_ge(hhi_ready, KD * s + k)
                        nc.vector.scalar_tensor_tensor(h_lo[:, k - 1, :], in0=tn[:, (k - 1) % 4, :],
                                                       scalar=modc[:, par, k - 1:k], in1=h_hi[:, k - 1, :].bitcast(F32),
                                                       op0=ALU.add, op1=ALU.subtract).then_inc(h_ready, 1)

            def residual(s, n, psum):
                gate = gate0[:, n:n + 1] if s == 0 else modc[:, s % 2, 16 + n:17 + n]
                nc.vector.scalar_tensor_tensor(xT[:, n, :], in0=psum, scalar=gate, in1=xT[:, n, :],
                                               op0=ALU.mult, op1=ALU.add).then_inc(x_ready, 1)

            def ffn_step(s, j, i=None):
                n, f = W0[s] + 3 * j, FFN_NO[s]
                up = n if j else n + 1
                done = FIT * f + j + 1
                if KINDS[s] == "conv":
                    def taps(q0):
                        dve.wait_ge(cv_ready, at(4 * j + q0 + 2, i, 8))
                        for back, c0, ready in ((1, C_CONVW[1], tap_done), (2, C_CONVW[0], conv_done)):
                            for q in (q0, q0 + 1):
                                tile = 2 * j + q % 2 + (FF // P) * (q // 2)
                                col = cols[:, c0 + tile:c0 + tile + 1] if i is None else cols[:, bass.ds(i * 4 + c0 + tile, 1)]
                                if back == 2:
                                    dve.wait_ge(tap_done, at(4 * j + q + 1, i, 8))
                                u = G[q // 2][:, T * (q % 2):T * (q % 2 + 1)]
                                nc.vector.scalar_tensor_tensor(cv[:, q, back:T], in0=u[:, 0:T - back], scalar=col,
                                                               in1=cv[:, q, back:T], op0=ALU.mult, op1=ALU.add
                                                               ).then_inc(ready, 1)

                    taps(0)
                    split_lo(n + 2, i)
                    taps(2)
                    dve.wait_ge(silu_ready, at(done, i, 2))
                    dve.wait_ge(conv_done, at(4 * j + 4, i, 8))
                    nc.vector.tensor_tensor(prod, sil[:, j % 2, :, :], cv[:, 2:4, :], ALU.mult).then_inc(mul_done, 1)
                else:
                    split_lo(n + 2, i)
                    dve.wait_ge(silu_ready, at(done, i, 2))
                    dve.wait_ge(unit_done, at(up + 1, i, 6))
                    nc.vector.tensor_tensor(prod.rearrange("p a b -> p (a b)"),
                                            sil[:, j % 2, :, :].rearrange("p a b -> p (a b)"), G[1][:, :],
                                            ALU.mult).then_inc(mul_done, 1)
                dve.wait_ge(mul_done, at(done, i, 2))
                nc.vector.tensor_copy(hid_hi[:, j % 2, :, :], prod).then_inc(hid_hi_done, 1)
                dve.wait_ge(hid_hi_done, at(done, i, 2))
                nc.vector.tensor_tensor(hid_lo[:, j % 2, :, :], prod, hid_hi[:, j % 2, :, :].bitcast(F32),
                                        ALU.subtract).then_inc(hid_ready, 1)
                if n + 3 < W0[-1]:
                    split_lo(n + 3, i)
                if N_ADA[s]:
                    ada_unit(s, j + 1, i)
                if n + 4 < W0[-1]:
                    split_lo(n + 4, i)

            def q_norm(s, u):
                kind = KINDS[s]
                q = QK_UNITS[kind].index(u)
                std_n = std[:, q % 2, :]
                dve.wait_ge(qstd_ready, QK0[s] + q + 1)
                nc.vector.reciprocal(std_n, std_n).then_inc(qrs_ready, 1)
                dve.wait_ge(qrs_ready, QK0[s] + q + 1)
                is_q, n = {"moba": (u < 2, u % 2), "swa": (u >= 2, u - 2 if u >= 2 else 0),
                           "fox": (u % 2 == 0, u // 2)}[kind]
                gain = C_GAIN + {"moba": 0, "swa": 2, "fox": 4}[kind] + (0 if is_q else 1)
                dst = (QT if is_q else KT)[:, 2 * n:2 * n + 2, :]
                split4 = lambda ap: ap.rearrange("p (a b) -> p a b", b=P)
                dst = split4(dst.rearrange("p a b -> p (a b)"))
                if is_q and kind != "fox":
                    dst = dst[:, :, ::-1]
                nc.vector.scalar_tensor_tensor(dst, in0=split4(G[u % 2][:, :]), scalar=cols[:, gain:gain + 1],
                                               in1=split4(std_n), op0=ALU.mult, op1=ALU.mult).then_inc(qk_ready, 1)

            def max_of(s, h):
                kind = KINDS[s]
                n = HEAD0[s] + h
                st, pr, L = stat[:, n % 3, :], P_of[n % 3], A[n % 2]
                first = 0.0
                b0, b1 = TB[:, h, P:2 * P], TB[:, h, :]
                if kind == "fox":
                    f0, f1 = tn[:, 0, 0:P], tn[:, 1, :]
                    if h % 2:
                        f0, f1 = tn[:, 2, 0:P], tn[:, 3, :]
                    nc.vector.scalar_tensor_tensor(f0, in0=TB[:, h, 0:P], scalar=Fq[:, 0, h:h + 1], in1=mask[:, P:2 * P],
                                                   op0=ALU.add, op1=ALU.add)
                    nc.vector.scalar_tensor_tensor(f1, in0=TB[:, h, :], scalar=Fq[:, 1, h:h + 1], in1=mask,
                                                   op0=ALU.add, op1=ALU.add).then_inc(bias_ready, 1)
                    b0, b1 = f0, f1
                    dve.wait_ge(bias_ready, h + 1)
                least = sink[:, h:h + 1] if kind == "swa" else LOWEST
                dve.wait_ge(qk_done, n + 1)
                if n >= 3:
                    dve.wait_ge(tr_done, n - 2)
                nc.vector.tensor_tensor_reduce(pr[:, 0:P], L[:, 0:P], b0, 1.0, least, ALU.add, ALU.max, st[:, 0:1])
                nc.vector.tensor_tensor_reduce(pr[:, P:384], L[:, P:384], b1, 1.0, least, ALU.add, ALU.max,
                                               st[:, 1:2]).then_inc(max_done, 1)
                dve.wait_ge(max_done, n + 1)
                ins = nc.vector.tensor_scalar(st[:, 2:4], st[:, 0:2], -1.0, None, ALU.mult)
                if kind == "swa":
                    ins.then_inc(neg_done, 1)
                    dve.wait_ge(neg_done, h + 1)
                    ins = nc.vector.tensor_scalar(st[:, 6:8], st[:, 2:4], sink[:, h:h + 1], None, ALU.add)
                ins.then_inc(am_done, 1)

            def normalise(s, h):
                n = HEAD0[s] + h
                st, pr = stat[:, n % 3, :], P_of[n % 3]
                dve.wait_ge(exp_done, n + 1)
                if KINDS[s] == "swa":
                    nc.vector.tensor_tensor(st[:, 4:6], st[:, 4:6], st[:, 6:8], ALU.add).then_inc(den_ready, 1)
                    dve.wait_ge(den_ready, HEAD0[s] + 2 * h + 1)
                nc.vector.reciprocal(st[:, 4:6], st[:, 4:6]).then_inc(den_ready, 1)
                dve.wait_ge(den_ready, n + 1 + (h + 1 if KINDS[s] == "swa" else 16 if KINDS[s] == "fox" else 0))
                nc.vector.tensor_scalar(pr[:, 0:P], pr[:, 0:P], st[:, 4:5], None, ALU.mult)
                nc.vector.tensor_scalar(pr[:, P:384], pr[:, P:384], st[:, 5:6], None, ALU.mult).then_inc(nm_done, 1)

            def out_lo(s, pair):
                n = HEAD0[s] // 2 + pair
                dve.wait_ge(ohi_done, n + 1)
                nc.vector.tensor_tensor(o_lo[:, pair, :], (A[3], S)[n % 2][:, 0:T], o_hi[:, pair, :].bitcast(F32),
                                        ALU.subtract).then_inc(olo_done, 1)

            def attention_step(s, t):
                nh = HEADS[KINDS[s]]
                if t < nh:
                    max_of(s, t)
                if 0 <= t - 1 < nh:
                    normalise(s, t - 1)
                if 0 <= t - 4 < nh and (t - 4) % 2:
                    out_lo(s, (t - 4) // 2)

            def out_units(s):
                kind = KINDS[s]
                for o in range(4):
                    u = OUT_UNITS[kind] + o
                    split_through(s, u + 2)
                    dve.wait_ge(unit_done, W0[s] + u + 1)
                    for n in range(2):
                        residual(s, 2 * o + n, G[o % 2][:, T * n:T * (n + 1)])

            def step(ins):
                nonlocal pool_steps
                pool_steps += 1
                ins.then_inc(pool_step, 1)
                dve.wait_ge(pool_step, pool_steps)

            def pool_branch(g):
                w = WINDOWS[g]
                src = V[:, g // 2, 512 + T * (g % 2):512 + T * (g % 2 + 1)]
                have, shift = src, 1
                n = 0
                while shift < w:
                    nxt = sq[:, n % 2, :]
                    nc.vector.tensor_copy(nxt[:, 0:shift], have[:, 0:shift])
                    step(nc.vector.tensor_tensor(nxt[:, shift:T], have[:, shift:T], have[:, 0:T - shift], ALU.add))
                    have, shift, n = nxt, 2 * shift, n + 1
                mean = sq[:, 2, 0:16]
                step(nc.vector.tensor_tensor(mean, have[:, 0:16], kon[:, K_INV + 16 * g:K_INV + 16 * (g + 1)], ALU.mult))
                dst = std[:, g // 2, T * (g % 2):T * (g % 2 + 1)]
                nc.vector.tensor_tensor(dst[:, 0:16], mean, src[:, 0:16], ALU.subtract)
                nc.vector.scalar_tensor_tensor(dst[:, 16:T], in0=have[:, 16:T], scalar=1.0 / w, in1=src[:, 16:T],
                                               op0=ALU.mult, op1=ALU.subtract).then_inc(pool_ready, 1)

            def merge(b, n):
                base = W0[0]
                at0 = 1024 * (n % 2)
                ma, mb = work[:, at0:at0 + 512], work[:, at0 + 512:at0 + 1024]
                flat = lambda ap: ap.rearrange("p a b -> p (a b)")
                gate_p = (QT if n < 2 else KT)[:, 4 + 2 * (n % 2):6 + 2 * (n % 2), :]
                dve.wait_ge(unit_done, base + (17 if n < 2 else 19))
                nc.vector.tensor_tensor(ma, A[b][:, :], flat(TB[:, 8 + 2 * n:10 + 2 * n, :]), ALU.mult).then_inc(merge_a, 1)
                dve.wait_ge(unit_done, base + (18 if n < 2 else 20))
                nc.vector.tensor_tensor(mb, A[2 + b][:, :], flat(gate_p), ALU.mult).then_inc(merge_b, 1)
                dve.wait_ge(merge_b, n + 1)
                nc.vector.tensor_tensor(ma, ma, mb, ALU.add).then_inc(merge_s, 1)
                dve.wait_ge(merge_s, n + 1)
                nc.vector.tensor_copy(flat(h_hi[:, 2 * n:2 * n + 2, :]), ma).then_inc(merge_hi, 1)
                dve.wait_ge(merge_hi, n + 1)
                nc.vector.tensor_tensor(flat(h_lo[:, 2 * n:2 * n + 2, :]), ma,
                                        flat(h_hi[:, 2 * n:2 * n + 2, :]).bitcast(F32), ALU.subtract).then_inc(merged, 1)

            nc.vector.memset(rows[:, :, :], 0.0).then_inc(rows_clear, 1)
            nc.vector.memset(ones[:, :], 1.0)
            nc.vector.memset(zeros[:, :], 0.0)
            nc.vector.memset(eps[:, :], EPS)
            nc.vector.memset(rel[:, :], 1.0).then_inc(ones_set, 1)
            dve.wait_ge(c_done, 1)
            ada_sum_of(0, 0)
            for b in range(4):
                dve.wait_ge(x_turned, b + 1)
                nc.vector.tensor_copy(xT[:, 2 * b:2 * b + 2, :].rearrange("p a b -> p (a b)"), A[b][:, :]).then_inc(x_ready, 2)
            ada_sum_of(1, 0)
            dve.wait_ge(rows_turned, 1)
            nc.vector.tensor_copy(cols[:, :], G[0][:, :]).then_inc(cols_done, 1)
            dve.wait_ge(cols_done, 1)
            nc.vector.tensor_scalar(cols[:, C_GAIN:C_GAIN + 6:2], cols[:, C_GAIN:C_GAIN + 6:2], HD ** -0.5, None,
                                    ALU.mult).then_inc(cols_done, 1)
            ada_sum_of(2, 0)
            for n in range(2):
                heads = (8, 16)[n]
                dve.wait_ge(bias_sum, n + 1)
                ins = nc.vector.tensor_copy(table_rows[0:heads, n, :], G[n][0:heads, 0:384])
            ins.then_inc(bias_rows, 1)
            for n in range(3, len(PRO_DVE)):
                ada_sum_of(n, 0)
            dve.wait_ge(f_hi_done, 1)
            nc.vector.tensor_tensor(f_lo[:, :, :], f_w[:, :, :], f_hi[:, :, :].bitcast(F32), ALU.subtract).then_inc(f_lo_done, 1)
            for s, kind in enumerate(KINDS):
                base = W0[s]
                norm_stats(s)
                if s == 0:
                    mod_columns(0)
                    split_through(0, 1)
                norm_apply(s)
                if kind in ("conv", "ffn"):
                    turns = PAIRS - (s == len(KINDS) - 1)
                    if N_ADA[s]:
                        ada_unit(s, 0)
                    ffn_step(s, 0)
                    with dve.Fori(0, turns) as i:
                        ffn_step(s, 1, i)
                        ffn_step(s, 2, i)
                    for j in range(1 + 2 * turns, FIT):
                        ffn_step(s, j)
                    next_lo = W0[s + 1] + 2
                    for n in range(KD):
                        if n in (0, 2, 4):
                            dve.wait_ge(acc_done, 3 * FFN_NO[s] + n // 2 + 1)
                        if n == 6:
                            dve.wait_ge(unit_done, W0[s + 1])
                        residual(s, n, A[n // 2][:, T * (n % 2):T * (n % 2 + 1)])
                elif kind == "moba":
                    for u in range(4):
                        split_through(s, u + 2)
                        q_norm(s, u)
                    split_through(s, 6)
                    dve.wait_ge(bias_in, 16)
                    for t in range(HEADS[kind] + 4):
                        attention_step(s, t)
                        if t == 2:
                            split_through(s, 7)
                        if t in (4, 6):
                            split_through(s, 8 + (t - 4) // 2)
                    dve.wait_ge(p_ready, 2)
                    for r in range(8):
                        split_through(s, 10 + r)
                        if r < 4:
                            pool_branch(r)
                        if r == 6:
                            pm = sq[:, :, :].rearrange("p a b -> p (a b)")
                            ph = o_hi[:, 4:8, :].rearrange("p a b -> p (a b)")
                            pl = o_lo[:, 4:8, :].rearrange("p a b -> p (a b)")
                            dve.wait_ge(ps_ready, 4)
                            nc.vector.tensor_copy(ph, pm).then_inc(phi_done, 1)
                            dve.wait_ge(phi_done, 1)
                            nc.vector.tensor_tensor(pl, pm, ph.bitcast(F32), ALU.subtract).then_inc(pool_split, 1)
                    split_through(s, 19)
                    dve.wait_ge(sig_ready, 8)
                    merge(0, 0)
                    merge(1, 1)
                    split_through(s, 21)
                    merge(0, 2)
                    merge(1, 3)
                    mod_columns(1)
                    out_units(s)
                elif kind == "swa":
                    split_through(s, 2)
                    q_norm(s, 0)
                    split_through(s, 3)
                    for u in range(2, 6):
                        split_through(s, u + 2)
                        q_norm(s, u)
                    dve.wait_ge(bias_in, 32)
                    for t in range(HEADS[kind] + 4):
                        attention_step(s, t)
                        if t == 4:
                            split_through(s, 8)
                    out_units(s)
                else:
                    for u in range(8):
                        split_through(s, u + 2)
                        if u == 1:
                            dve.wait_ge(fl_done, 1)
                            nc.vector.tensor_tensor(fz[:, 0, :], A[0][:, 0:32], fb[:, :, :].rearrange("p a b -> p (a b)"),
                                                    ALU.add).then_inc(fz_ready, 1)
                            dve.wait_ge(fz_ready, 1)
                            nc.vector.scalar_tensor_tensor(fz[:, 1, :], in0=fz[:, 0, :], scalar=-1.0, in1=fz[:, 0, :],
                                                           op0=ALU.mult, op1=ALU.min).then_inc(fz_ready, 1)
                            dve.wait_ge(f_ln, 1)
                            nc.vector.scalar_tensor_tensor(fz[:, 4, :], in0=fz[:, 0, :], scalar=0.0, in1=fz[:, 3, :],
                                                           op0=ALU.min, op1=ALU.subtract).then_inc(lf_ready, 1)
                        if u == 3:
                            dve.wait_ge(cum_done, 1)
                            nc.vector.tensor_copy(Fq[:, :, :].rearrange("p a b -> p (a b)"), A[1][:, 0:32]).then_inc(fq_ready, 1)
                        if u == 5:
                            dve.wait_ge(ft_done, 1)
                            nc.vector.tensor_scalar(nFT[:, :], A[2][0:16, 0:T], -1.0, None, ALU.mult).then_inc(nft_ready, 1)
                        q_norm(s, u)
                    split_through(s, 10)
                    dve.wait_ge(bias_in, 48)
                    for t in range(HEADS[kind] + 4):
                        attention_step(s, t)
                        if t in (3, 7, 11):
                            u = 11 + (t - 3) // 4
                            split_through(s, u)
                    out_units(s)
                if s + 1 < len(KINDS) and s > 0:
                    mod_columns(s + 1)
            for b in range(4):
                dve.wait_ge(y_turned, b + 1)
                nc.vector.tensor_copy(V[:, b // 2, 512 * (b % 2):512 * (b % 2 + 1)], (G[0], G[1], M, S)[b][:, :]).then_inc(y_ready, 1)

        @block.tensor
        def _(pe):
            mm = nc.tensor.matmul

            def product(outp, wh, wl, xh, xl, start, stop):
                mm(outp, wh, xh, start=start, stop=False, skip_group_check=True)
                mm(outp, wh, xl, start=False, stop=False, skip_group_check=True)
                return mm(outp, wl, xh, start=False, stop=stop, skip_group_check=True)

            def unit_of(w, tiles):
                s = split_of(w)
                cut = lambda ap: ap[:, s, :].rearrange("p (k n) -> p k n", k=tiles)
                return cut(hi), cut(lo)

            def half(w, bank, n, xh=h_hi, xl=h_lo, last=True):
                if n == 0:
                    pe.wait_ge(lo_ready, w + 1)
                wh, wl = unit_of(w, KD)
                for k in range(KD):
                    ins = product(bank[:, T * n:T * (n + 1)], wh[:, k, P * n:P * (n + 1)], wl[:, k, P * n:P * (n + 1)],
                                  xh[:, k, :], xl[:, k, :], k == 0, k == KD - 1)
                if n == 1:
                    ins.then_inc(unit_done, 1)

            def unit(w, bank, i=None, **kw):
                pe.wait_ge(lo_ready, at(w + 1, i, 6))
                wh, wl = unit_of(w, KD)
                for n in range(2):
                    for k in range(KD):
                        ins = product(bank[:, T * n:T * (n + 1)], wh[:, k, P * n:P * (n + 1)],
                                      wl[:, k, P * n:P * (n + 1)], h_hi[:, k, :], h_lo[:, k, :], k == 0, k == KD - 1)
                ins.then_inc(unit_done, 1)

            def first_unit(s, bank):
                w = W0[s]
                pe.wait_ge(lo_ready, w + 1)
                wh, wl = unit_of(w, KD)
                for k in range(KD):
                    pe.wait_ge(h_ready, KD * s + k + 1)
                    for n in range(2):
                        ins = product(bank[:, T * n:T * (n + 1)], wh[:, k, P * n:P * (n + 1)],
                                      wl[:, k, P * n:P * (n + 1)], h_hi[:, k, :], h_lo[:, k, :],
                                      k == 0 and n == 0, k == KD - 1)
                ins.then_inc(unit_done, 1)

            def v_half(w, bank, n):
                if n == 0:
                    pe.wait_ge(lo_ready, w + 1)
                wh, wl = unit_of(w, KD)
                for k in range(KD):
                    ins = product(bank[:, CW * n:CW * (n + 1)], h_hi[:, k, P * n:P * (n + 1)],
                                  h_lo[:, k, P * n:P * (n + 1)], wh[:, k, :], wl[:, k, :], k == 0, k == KD - 1)
                if n == 1:
                    ins.then_inc(unit_done, 1)

            def ada_reduce(s, b, i=None):
                if b == 0:
                    pe.wait_ge(mod_ready, 2 * s + 2)
                sum_partitions(A0[s] + b, 2 * b, i)

            def sum_partitions(n, col, i=None):
                pe.wait_ge(ada_ready, at(n + 1, i, 2))
                for c in range(2):
                    dst = M[:, col + c:col + c + 1] if i is None else M[:, bass.ds(i * 4 + col + c, 1)]
                    ins = mm(dst, ada_sum[:, n % 2, P * c:P * (c + 1)], ones[:, 0:1], start=True, stop=True)
                ins.then_inc(ada_used, 1)

            def norm(s):
                for k in range(KD):
                    pe.wait_ge(sq_ready, KD * s + k + 1)
                    ins = mm(S[:, 0:T], ones[:, :], sq[:, k % 4, :], start=k == 0, stop=k == KD - 1)
                    if k < KD - 1:
                        ins.then_inc(sq_used, 1)
                ins.then_inc(stats_done, 1)

            def down(w, step, order, i=None):
                pe.wait_ge(lo_ready, at(w + 1, i, 6))
                wh, wl = unit_of(w, 2)
                last = order == "tiles first"
                for n, k in ([(n, k) for n in range(KD) for k in range(2)] if last else
                             [(n, k) for k in range(2) for n in range(KD)]):
                    ins = product(A[n // 2][:, T * (n % 2):T * (n % 2 + 1)], wh[:, k, P * n:P * (n + 1)],
                                  wl[:, k, P * n:P * (n + 1)], hid_hi[:, step % 2, k, :], hid_lo[:, step % 2, k, :],
                                  False, last and k == 1)
                    if last and k == 1 and n in (1, 3, 5):
                        ins.then_inc(acc_done, 1)
                ins.then_inc(unit_done, 1)

            def ffn(s):
                base, f, conv = W0[s], FFN_NO[s], KINDS[s] == "conv"
                for b in range(4):
                    mm(A[b][:, :], zeros[:, 0:P], zeros[:, :], start=True, stop=False, skip_group_check=True)
                first_unit(s, G[0])
                unit(base + 1, G[1])
                if N_ADA[s]:
                    ada_reduce(s, 0)
                with pe.Fori(0, PAIRS) as i:
                    for e in range(2):
                        j = e + 1
                        u = base + 3 * j - 1
                        if conv:
                            pe.wait_ge(conv_done, at(4 * j - 2, i, 8))
                        else:
                            pe.wait_ge(mul_done, at(FIT * f + j, i, 2))
                        unit(u, G[0], i)
                        if conv:
                            pe.wait_ge(conv_done, at(4 * j, i, 8))
                        unit(u + 1, G[1], i)
                        if N_ADA[s]:
                            ada_reduce(s, j, i)
                        pe.wait_ge(hid_ready, at(FIT * f + j, i, 2))
                        down(u + 2, j - 1, "rows first", i)
                pe.wait_ge(hid_ready, FIT * (f + 1))
                down(base + 3 * FIT - 1, FIT - 1, "tiles first")

            def q_sums(s, q):
                pe.wait_ge(qsq_ready, QK0[s] + q + 1)
                if q:
                    pe.wait_ge(qstd_ready, QK0[s] + q)
                mm(S[:, :], head_ones, sq[:, 2 * (q % 2):2 * (q % 2) + 2, :].rearrange("p a b -> p (a b)"),
                   start=True, stop=True).then_inc(qs_done, 1)

            def logits(s, h):
                n = HEAD0[s] + h
                if n >= 2:
                    pe.wait_ge(am_done, n - 1)
                L, row = A[n % 2], HD * (h % 2)
                q = QT[row:row + HD, h // 2, :]
                k = (KT[row:row + HD, 4 + h // 4, :] if KINDS[s] == "swa" else KT[row:row + HD, h // 2, :])
                mm(L[:, 0:P], q[:, 0:P], k[:, 0:P], start=True, stop=True)
                mm(L[:, P:384], q[:, P:T], k, start=True, stop=True).then_inc(qk_done, 1)

            def turn(s, h):
                n = HEAD0[s] + h
                pe.wait_ge(nm_done, n + 1)
                if n:
                    pe.wait_ge(ptc_done, n)
                for c in range(3):
                    ins = nc.tensor.transpose(A[2][:, P * c:P * (c + 1)], P_of[n % 3][:, P * c:P * (c + 1)], ident)
                ins.then_inc(tr_done, 1)

            def values(s, h):
                n = HEAD0[s] + h
                pair = n // 2
                pe.wait_ge(ptc_done, n + 1)
                if h % 2 == 0 and pair >= 2:
                    pe.wait_ge(olo_done, pair - 1)
                v = h // 4 if KINDS[s] == "swa" else h
                if (KINDS[s] == "swa" and h == 0) or (KINDS[s] != "swa" and h % 4 == 0):
                    pe.wait_ge(v_ready, V0[s] + v // 4 + 1)
                row = HD * (h % 2)
                Z, pt = (A[3], S)[pair % 2], PT_of[n % 2]
                mm(Z[row:row + HD, 0:T], V[:, 0, HD * v:HD * (v + 1)], pt[:, 0:T], start=True, stop=False,
                   skip_group_check=True)
                mm(Z[row:row + HD, P:T], V[:, 1, HD * v:HD * (v + 1)], pt[:, T:384], start=False, stop=True,
                   skip_group_check=True).then_inc(pv_done, 1)

            def attention_step(s, t):
                nh = HEADS[KINDS[s]]
                if t < nh:
                    logits(s, t)
                if 0 <= t - 2 < nh:
                    turn(s, t - 2)
                if 0 <= t - 3 < nh:
                    values(s, t - 3)

            reduced = [0] * len(KINDS)

            def reduces(s, u):
                while reduced[s] < N_ADA[s] and ADA_AFTER[KINDS[s]][reduced[s]] <= u:
                    ada_reduce(s, reduced[s])
                    reduced[s] += 1

            def q_unit(s, u, bank):
                kind = KINDS[s]
                q_before = QK_UNITS[kind].index(u - 1) if u - 1 in QK_UNITS[kind] else None
                reduces(s, u)
                if u >= 2 and u - 2 in QK_UNITS[kind]:
                    pe.wait_ge(qk_ready, QK0[s] + QK_UNITS[kind].index(u - 2) + 1)
                if kind == "swa" and u == 3:
                    pe.wait_ge(v_ready, V0[s] + 1)
                do = v_half if u in V_UNITS[kind] else half
                do(W0[s] + u, bank, 0)
                if q_before is not None:
                    q_sums(s, q_before)
                do(W0[s] + u, bank, 1)

            def out_units(s, xh, xl):
                kind = KINDS[s]
                for o in range(4):
                    u = OUT_UNITS[kind] + o
                    reduces(s, u)
                    if o >= 2:
                        pe.wait_ge(x_ready, KD * (s + 1) + 2 * (o - 1))
                    half(W0[s] + u, G[o % 2], 0, xh, xl)
                    half(W0[s] + u, G[o % 2], 1, xh, xl)
                reduces(s, NUNITS[kind] + 1)

            def direct(n):
                r = PRO_PE[n]
                pe.wait_ge(raw_full[n], 16)
                w = raw[:, n, :].rearrange("p (k n) -> p k n", k=KD)
                for c in range(2):
                    for k in range(KD):
                        ins = mm(M[:, 2 * r + c:2 * r + c + 1], w[:, k, P * c:P * (c + 1)], c_act[:, k:k + 1],
                                 start=k == 0, stop=k == KD - 1)
                ins.then_inc(pro_done, 1)

            def pro_reduce(n):
                sum_partitions(n, 2 * PRO_DVE[n])

            pe.wait_ge(c_full, 48)
            nc.tensor.transpose(S[:, 0:16], c_rows[:, :], ident[0:16, 0:16]).then_inc(c_turned, 1)
            pe.wait_ge(c_done, 1)
            direct(0)
            pe.wait_ge(x_full, 16)
            for k in range(KD):
                for t in range(2):
                    ins = nc.tensor.transpose(A[k // 2][:, T * (k % 2) + P * t:T * (k % 2) + P * (t + 1)],
                                              x_in[:, t, P * k:P * (k + 1)], ident)
                if k % 2:
                    ins.then_inc(x_turned, 1)
            pe.wait_ge(rows_full, ROWS_LOADED)
            for t in range(4):
                ins = nc.tensor.transpose(G[0][:, P * t:P * (t + 1)], rows[:, t, :], ident)
            ins.then_inc(rows_turned, 1)
            pro_reduce(0)
            pe.wait_ge(small_full, SMALL_LOADED)
            pe.wait_ge(ones_set, 1)
            pe.wait_ge(cols_done, 2)
            for n in range(2):
                heads = (8, 16)[n]
                mm(G[n][0:heads, 0:384], rel[0:33, 8 * n:8 * n + heads], tables[:, 384 * n:384 * (n + 1)],
                   start=True, stop=True).then_inc(bias_sum, 1)
            norm(0)
            pro_reduce(1)
            direct(1)
            for n in range(2, len(PRO_DVE)):
                pro_reduce(n)

            for s, kind in enumerate(KINDS):
                base = W0[s]
                if s:
                    norm(s)
                if kind in ("conv", "ffn"):
                    ffn(s)
                    if N_ADA[s]:
                        ada_reduce(s, 11)
                elif kind == "moba":
                    first_unit(s, G[0])
                    for u in range(1, 5):
                        q_unit(s, u, G[u % 2])
                    for t in range(HEADS[kind] + 3):
                        if t == 0:
                            pe.wait_ge(qk_ready, QK0[s] + 4)
                        attention_step(s, t)
                        if t < 6:
                            u = 5 + t // 2
                            if t % 2 == 0:
                                reduces(s, u)
                            if u == 5:
                                v_half(base + u, G[u % 2], t % 2)
                            else:
                                if t == 2:
                                    pe.wait_ge(v_ready, V0[s] + 1)
                                if t == 4:
                                    pe.wait_ge(v_ready, V0[s] + 2)
                                half(base + u, G[u % 2], t % 2)
                    for r in range(8):
                        reduces(s, 8 + r)
                        if r < 2:
                            pe.wait_ge(p_ready, r + 1)
                        else:
                            pe.wait_ge(sig_ready, r - 1)
                        half(base + 8 + r, G[r % 2], 0)
                        half(base + 8 + r, G[r % 2], 1)
                        if r == 5:
                            pe.wait_ge(pool_ready, 4)
                            for g in range(4):
                                mm(A[g // 2][:, T * (g % 2):T * (g % 2 + 1)], pool_w[:, g, :],
                                   std[:, g // 2, T * (g % 2):T * (g % 2 + 1)], start=True, stop=True).then_inc(pw_done, 1)
                    pe.wait_ge(pool_split, 1)
                    for m in range(4):
                        u = 16 + m
                        reduces(s, u)
                        if m >= 2:
                            pe.wait_ge((merge_a, merge_b)[m % 2], 2)
                        pe.wait_ge(lo_ready, base + u + 1)
                        wh, wl = unit_of(base + u, 4)
                        x0 = 4 * (m % 2)
                        for n in range(4):
                            for k in range(4):
                                ins = product(A[2 * (m % 2) + n // 2][:, T * (n % 2):T * (n % 2 + 1)],
                                              wh[:, k, P * n:P * (n + 1)], wl[:, k, P * n:P * (n + 1)],
                                              o_hi[:, x0 + k, :], o_lo[:, x0 + k, :], k == 0, k == 3)
                        ins.then_inc(unit_done, 1)
                    reduces(s, 21)
                    pe.wait_ge(merged, 4)
                    out_units(s, h_hi, h_lo)
                elif kind == "swa":
                    first_unit(s, G[0])
                    for u in range(1, 6):
                        if u == 3:
                            pe.wait_ge(qk_ready, QK0[s] + 1)
                            for g in range(4):
                                dup = kon[:, K_DUP + P * (g % 2):K_DUP + P * (g % 2 + 1)]
                                ins = mm(A[g // 2][:, T * (g % 2):T * (g % 2 + 1)], dup, KT[:, g // 2, :], start=True, stop=True)
                                if g % 2:
                                    ins.then_inc(dup_done, 1)
                        q_unit(s, u, G[u % 2])
                    reduces(s, 6)
                    q_sums(s, 4)
                    pe.wait_ge(dup_ready, 2)
                    pe.wait_ge(qk_ready, QK0[s] + 5)
                    for t in range(HEADS[kind] + 3):
                        attention_step(s, t)
                    pe.wait_ge(olo_done, (HEAD0[s] + HEADS[kind]) // 2)
                    out_units(s, o_hi, o_lo)
                else:
                    first_unit(s, G[0])
                    pe.wait_ge(f_lo_done, 1)
                    for t in range(2):
                        for k in range(KD):
                            ins = product(A[0][:, 16 * t:16 * (t + 1)], h_hi[:, k, P * t:P * (t + 1)],
                                          h_lo[:, k, P * t:P * (t + 1)], f_hi[:, k, :], f_lo[:, k, :], k == 0, k == KD - 1)
                    ins.then_inc(fl_done, 1)
                    for u in range(1, 9):
                        if u == 4:
                            pe.wait_ge(lf_ready, 1)
                            lf = fz[:, 4, :]
                            mm(A[1][:, 0:16], tri, lf[:, 0:16], start=True, stop=True)
                            mm(A[1][:, 16:32], ones[:, :], lf[:, 0:16], start=True, stop=False)
                            mm(A[1][:, 16:32], tri, lf[:, 16:32], start=False, stop=True).then_inc(cum_done, 1)
                        if u == 6:
                            pe.wait_ge(fq_ready, 1)
                            for t in range(2):
                                ins = nc.tensor.transpose(A[2][0:16, P * t:P * (t + 1)], Fq[:, t, :], ident)
                            ins.then_inc(ft_done, 1)
                        q_unit(s, u, G[u % 2])
                    pe.wait_ge(qk_ready, QK0[s] + 8)
                    for t in range(HEADS[kind] + 3):
                        attention_step(s, t)
                        if t in (1, 2, 5, 6, 9, 10):
                            u = 9 + t // 4
                            n = (t - 1) % 4
                            if n == 0:
                                reduces(s, u)
                                if u > 9:
                                    pe.wait_ge(v_ready, V0[s] + u - 9)
                            v_half(base + u, G[u % 2], n)
                    reduces(s, 12)
                    pe.wait_ge(olo_done, (HEAD0[s] + HEADS[kind]) // 2)
                    out_units(s, o_hi, o_lo)
            for b in range(4):
                pe.wait_ge(x_ready, KD * len(KINDS) + 4 * (b % 2) + 4)
                for k in range(4):
                    ins = nc.tensor.transpose((G[0], G[1], M, S)[b][:, P * k:P * (k + 1)],
                                              xT[:, 4 * (b % 2) + k, P * (b // 2):P * (b // 2 + 1)], ident)
                ins.then_inc(y_turned, 1)


def constants():
    k = np.zeros((P, K_END), np.float32)
    i, j = np.arange(P)[:, None], np.arange(P)[None, :]
    k[:, K_IDENT:K_IDENT + P] = i == j
    k[:, K_HEADS:K_HEADS + P] = i // HD == j // HD
    k[:, K_TRI:K_TRI + P] = i <= j
    k[:, K_MASK + P:K_MASK + 2 * P] = np.where(j <= i, 0.0, NEG)
    for h in range(2):
        k[:, K_DUP + P * h:K_DUP + P * (h + 1)] = i == j % HD + HD * h
    for g, w in enumerate(WINDOWS):
        k[:, K_INV + 16 * g:K_INV + 16 * (g + 1)] = 1.0 / np.minimum(np.arange(16) + 1, w)
    return k


def bucket_tables():
    t = np.zeros((33, 2, 384), np.float32)
    for n, window in enumerate((T, P)):
        for x in range(384):
            d = T - 1 - x
            if not 0 <= d < window:
                t[32, n, x] = NEG
            elif d < 16:
                t[d, n, x] = 1.0
            else:
                t[min(16 + int(np.log(d / 16) / np.log(128 / 16) * 16), 31), n, x] = 1.0
    return t.reshape(33, 768)


def kernel(**inputs):
    import concourse.bacc as bacc
    from concourse.bass_utils import run_bass_kernel_spmd

    nc = bacc.Bacc("TRN2", target_bir_lowering=False, num_devices=1)
    arrays, aps = {}, {}
    for name, value in {**inputs, "constants": constants(), "bucket_tables": bucket_tables()}.items():
        value = np.ascontiguousarray(value)
        arrays[f"in_{name}"] = value
        aps[name] = nc.dram_tensor(f"in_{name}", value.shape, mybir.dt.from_np(value.dtype), kind="ExternalInput").ap()
    out = nc.dram_tensor("out", (1, T, D), F32, kind="ExternalOutput").ap()
    build(nc, aps, aps["constants"], aps["bucket_tables"], out)
    r = run_bass_kernel_spmd(nc, [arrays], core_ids=[0])
    return r.results[0]["out"]
```

```python
from contextlib import ExitStack

import numpy as np

import concourse.bass as bass
from concourse import mybir

F32 = mybir.dt.float32
F32R = mybir.dt.float32r
BF16 = mybir.dt.bfloat16
ALU = mybir.AluOpType
ACT = mybir.ActivationFunctionType

P = 128
D = 1024
T = 256
KD = D // P
FF = 2816
HD = 64
UNIT = 2048
CW = 256
NBUF = 3
PRO_PE = [0, 2]
PRO_DVE = [1, 3, 4, 5, 6, 7]
PRO = len(PRO_PE)
FIT = FF // CW
PAIRS = (FIT - 1) // 2
EPS = 1e-6
NEG = -1e30
LOWEST = -3e38

KINDS = ["moba", "conv", "ffn", "swa", "ffn", "ffn", "fox", "ffn"]
NUNITS = {"moba": 24, "conv": 3 * FIT, "ffn": 3 * FIT, "swa": 10, "fox": 16}
N_ADA = [16, 12, 12, 12, 12, 12, 12, 0]
W0 = [sum(NUNITS[k] for k in KINDS[:s]) for s in range(len(KINDS) + 1)]
A0 = [len(PRO_DVE) + sum(N_ADA[:s]) for s in range(len(KINDS) + 1)]
FFN_NO = [sum(k in ("conv", "ffn") for k in KINDS[:s]) for s in range(len(KINDS))]
HEADS = {"moba": 8, "swa": 16, "fox": 16}
HEAD0 = [sum(HEADS.get(k, 0) for k in KINDS[:s]) for s in range(len(KINDS))]
QK_UNITS = {"moba": [0, 1, 2, 3], "swa": [0, 2, 3, 4, 5], "fox": list(range(8))}
QK0 = [sum(len(QK_UNITS.get(k, [])) for k in KINDS[:s]) for s in range(len(KINDS))]
V_UNITS = {"moba": [4, 5], "swa": [1], "fox": [8, 9, 10, 11]}
V0 = [sum(len(V_UNITS.get(k, [])) for k in KINDS[:s]) for s in range(len(KINDS))]
OUT_UNITS = {"moba": 20, "swa": 6, "fox": 12}
ADA_AFTER = {
    "moba": [1, 2, 3, 4, 5, 6, 7, 8, 9, 10, 11, 12, 13, 14, 15, 20],
    "swa": [2, 3, 4, 5, 6, 6, 6, 6, 8, 9, 9, 10],
    "fox": [2, 4, 5, 6, 7, 8, 9, 9, 9, 13, 14, 15],
}

DIRECT = {"moba": [6, 7, 8, 15], "swa": [4, 5, 6, 7], "fox": [6, 7, 8]}
QUARTERS = {
    "moba": [4, 5, 6, 6, 7, 7, 8, 8, 9, 9, 10, 10],
    "swa": list(range(1, 17)),
    "fox": [3, 4, 7, 8, 11, 12, 13, 14, 15, 16, 17, 18],
}
DIRECT_UNITS = [A0[s] + b for s, kind in enumerate(KINDS) for b in DIRECT.get(kind, [])]


def taken_by_pe(n):
    return sum(m < n for m in DIRECT_UNITS)


def taken_by_dve(n):
    return n - taken_by_pe(n)


C_ADAB, C_N1, C_N2, C_NG2 = 0, 64, 72, 80
C_ADAB2, C_CONVB, C_PSCALE, C_GAIN = (128, 256), 200, 244, 248
C_CONVW = (328, 384, 428)

K_IDENT, K_HEADS, K_TRI, K_MASK, K_DUP, K_INV, K_END = 0, 128, 256, 384, 640, 896, 960
WINDOWS = (2, 4, 8, 16)
ROWS_LOADED = 23 * 16
SMALL_LOADED = 9 * 16


def at(base, i=None, per=0):
    return base if i is None else i * per + base


def build(nc, a, consts, buckets, out):
    ctx = ExitStack()
    with ctx:
        def sb(name, shape, dt=F32):
            return ctx.enter_context(nc.sbuf_tensor(name, shape, dt))

        def sem(name):
            return ctx.enter_context(nc.semaphore(name))

        raw = sb("raw", [P, NBUF, UNIT])
        hi = sb("hi", [P, NBUF, UNIT], F32R)
        lo = sb("lo", [P, NBUF, UNIT], F32R)
        ada = sb("ada", [P, 2, KD, CW])
        ada_sum = sb("ada_sum", [P, 2, CW])
        xT = sb("xT", [P, KD, T])
        h_hi = sb("h_hi", [P, KD, T], F32R)
        h_lo = sb("h_lo", [P, KD, T], F32R)
        QT = sb("QT", [P, 8, T])
        KT = sb("KT", [P, 8, T])
        V = sb("V", [P, 2, D])
        o_hi = sb("o_hi", [P, 8, T], F32R)
        o_lo = sb("o_lo", [P, 8, T], F32R)
        TB = sb("TB", [P, 16, T])
        sq = sb("sq", [P, 4, T])
        std = sb("std", [P, 2, 512])
        hstd = sb("hstd", [P, 2, 8])
        tn = sb("tn", [P, 4, T])
        work = sb("work", [P, 2048])
        cols = sb("cols", [P, 512])
        kon = sb("kon", [P, K_END])
        ones = sb("ones", [P, P])
        zeros = sb("zeros", [P, 512], BF16)
        pool_w = sb("pool_w", [P, 4, P])
        f_w = sb("f_w", [P, KD, 16])
        f_hi = sb("f_hi", [P, KD, 16], F32R)
        f_lo = sb("f_lo", [P, KD, 16], F32R)
        c_act = sb("c_act", [P, 16])
        modc = sb("modc", [P, 2, 24])
        acol = sb("acol", [P, 2, 8])
        gate0 = sb("gate0", [P, 8])
        eps = sb("eps", [P, 1])
        stat = sb("stat", [P, 3, 8])
        sink = sb("sink", [P, 16])
        c_rows = sb("c_rows", [16, P])
        warm = sb("warm", [P, 1])
        fb = sb("fb", [P, 2, 16])
        fz = sb("fz", [P, 5, 32])
        Fq = sb("Fq", [P, 2, 16])
        nFT = sb("nFT", [16, T])
        rel = sb("rel", [64, 24])

        banks = [ctx.enter_context(nc.psum_tensor(f"bank{b}", [P, 512], F32)) for b in range(8)]
        A, G, M, S = banks[0:4], banks[4:6], banks[6], banks[7]

        ident = kon[:, K_IDENT:K_IDENT + P]
        head_cols = kon[:, K_HEADS:K_HEADS + 2]
        tri = kon[:, K_TRI:K_TRI + P]
        mask = kon[:, K_MASK:K_MASK + 2 * P]
        P_of = [work[:, 384 * n:384 * n + 384] for n in range(3)]
        PT_of = [work[:, 1152 + 384 * n:1536 + 384 * n] for n in range(2)]
        hid_hi = o_hi[:, 0:4, :].rearrange("p (a b) t -> p a b t", a=2)
        hid_lo = o_lo[:, 0:4, :].rearrange("p (a b) t -> p a b t", a=2)
        cv = QT[:, 0:4, :]
        sil = KT[:, 0:4, :].rearrange("p (a b) t -> p a b t", a=2)
        prod = KT[:, 4:6, :]
        rows = TB[:, 0:2, :].rearrange("p a (b c) -> p (a b) c", b=2)
        x_in = V
        tables = tn[0:33, 0:3, :].rearrange("p a b -> p (a b)")
        table_rows = V[0:16, 0, 0:768].rearrange("p (a b) -> p a b", a=2)

        scratch = nc.dram_tensor("bias_by_distance", (2, 16, 384), F32).ap()
        scratch_f = nc.dram_tensor("forget_rows", (16, T), F32).ap()

        raw_full = [sem(f"raw_full{n}") for n in range(NBUF)]
        ada_full = [sem(f"ada_full{n}") for n in range(2)]
        rows_full, small_full, x_full = sem("rows_full"), sem("small_full"), sem("x_full")
        c_full, c_turned = sem("c_full"), sem("c_turned")
        rows_clear = sem("rows_clear")
        bias_out, bias_in = sem("bias_out"), sem("bias_in")
        forget_out, stored = sem("forget_out"), sem("stored")
        ones_set, cols_done, c_done = sem("ones_set"), sem("cols_done"), sem("c_done")
        rows_turned, x_turned = sem("rows_turned"), sem("x_turned")
        bias_sum, bias_rows = sem("bias_sum"), sem("bias_rows")
        pro_done = sem("pro_done")
        f_hi_done, f_lo_done = sem("f_hi_done"), sem("f_lo_done")
        hi_ready, lo_ready, unit_done = sem("hi_ready"), sem("lo_ready"), sem("unit_done")
        ada_step, ada_ready, ada_used = sem("ada_step"), sem("ada_ready"), sem("ada_used")
        ada_direct = sem("ada_direct")
        mod_ready = sem("mod_ready")
        x_ready, sq_ready, sq_used = sem("x_ready"), sem("sq_ready"), sem("sq_used")
        stats_done, std_ready, rstd_ready = sem("stats_done"), sem("std_ready"), sem("rstd_ready")
        t_ready, hhi_ready, h_ready = sem("t_ready"), sem("hhi_ready"), sem("h_ready")
        acc_zero, acc_done = sem("acc_zero"), sem("acc_done")
        cv_ready, tap_done, conv_done = sem("cv_ready"), sem("tap_done"), sem("conv_done")
        silu_ready, mul_done = sem("silu_ready"), sem("mul_done")
        hid_hi_done, hid_ready = sem("hid_hi_done"), sem("hid_ready")
        qsq_ready, qs_done, qstd_ready = sem("qsq_ready"), sem("qs_done"), sem("qstd_ready")
        qrs_ready, qb_done, qc_ready = sem("qrs_ready"), sem("qb_done"), sem("qc_ready")
        qk_ready, v_ready = sem("qk_ready"), sem("v_ready")
        p_ready, sig_ready = sem("p_ready"), sem("sig_ready")
        dup_done, dup_ready = sem("dup_done"), sem("dup_ready")
        fl_done, fz_ready, f_exp, f_ln = sem("fl_done"), sem("fz_ready"), sem("f_exp"), sem("f_ln")
        lf_ready, cum_done, fq_ready = sem("lf_ready"), sem("cum_done"), sem("fq_ready")
        ft_done, nft_ready = sem("ft_done"), sem("nft_ready")
        qk_done, bias_ready, max_done = sem("qk_done"), sem("bias_ready"), sem("max_done")
        neg_done, am_done, exp_done = sem("neg_done"), sem("am_done"), sem("exp_done")
        den_ready, nm_done, tr_done = sem("den_ready"), sem("nm_done"), sem("tr_done")
        ptc_done, pv_done = sem("ptc_done"), sem("pv_done")
        ohi_done, olo_done = sem("ohi_done"), sem("olo_done")
        pool_step, pool_ready, pw_done = sem("pool_step"), sem("pool_ready"), sem("pw_done")
        ps_ready, phi_done, pool_split = sem("ps_ready"), sem("phi_done"), sem("pool_split")
        merge_a, merge_b, merge_s = sem("merge_a"), sem("merge_b"), sem("merge_s")
        merge_hi, merged = sem("merge_hi"), sem("merged")
        y_turned, y_ready = sem("y_turned"), sem("y_ready")

        def bank_of(s, u):
            return (G[0], G[1], A[2], A[3])[u % 4] if u in QK_UNITS[KINDS[s]] else G[u % 2]

        def split_of(w):
            return w % NBUF

        def raw_of(w):
            return (w + PRO) % NBUF

        def all_rows(ap):
            return ap.rearrange("(k p) n -> p k n", p=P)


        ada_1 = all_rows(a["ada_w"][0])

        def ada_source(s, b):
            if s == 0:
                return ada_1[:, :, 2 * D + CW * b:2 * D + CW * (b + 1)]
            l, stage = divmod(s - 1, 3)
            first = 3 * D * stage
            src = all_rows(a["ada_w_2"][l])
            if isinstance(b, int):
                return src[:, :, first + CW * b:first + CW * (b + 1)]
            return src[:, :, bass.ds(b * CW + first, CW)]

        def unit_source(s, m):
            kind = KINDS[s]
            if kind == "moba":
                w_in = all_rows(a["w_in"][0])
                if m < 16:
                    return w_in[:, :, CW * m:CW * (m + 1)], KD
                if m < 20:
                    w = a["w_branch_attn"][0] if m % 2 == 0 else a["w_branch_pool"][0]
                    half = (m - 16) // 2
                    return all_rows(w)[:, :, 512 * half:512 * (half + 1)], 4
                return all_rows(a["w_out"][0])[:, :, CW * (m - 20):CW * (m - 19)], KD
            if kind == "swa":
                if m < 6:
                    c = [4, 5, 0, 1, 2, 3][m]
                    return all_rows(a["swa_w_in_2"][0])[:, :, CW * c:CW * (c + 1)], KD
                return all_rows(a["swa_w_out_2"][0])[:, :, CW * (m - 6):CW * (m - 5)], KD
            if m < 12:
                c = m // 2 + 4 * (m % 2) if m < 8 else m
                return all_rows(a["fox_w_in_2"][0])[:, :, CW * c:CW * (c + 1)], KD
            return all_rows(a["fox_w_out_2"][0])[:, :, CW * (m - 12):CW * (m - 11)], KD

        def ffn_weights(s):
            if KINDS[s] == "conv":
                return a["w_up"][0], a["w_down"][0]
            l, n = {2: (0, 0), 4: (0, 1), 5: (1, 0), 7: (1, 1)}[s]
            return a["ffn_w13_2"][l, n], a["ffn_w2_2"][l, n]

        block = ctx.enter_context(nc.Block())

        @block.sync
        def _(sp):
            def load(w, src, tiles, i=None):
                if w >= NBUF:
                    sp.wait_ge(lo_ready, at(w - NBUF + 1, i, 6))
                elif w + PRO >= NBUF:
                    sp.wait_ge(pro_done, w + PRO - NBUF + 1)
                dst = raw[:, raw_of(w), :].rearrange("p (k n) -> p k n", k=tiles)
                sp.dma_start(dst, src).then_inc(raw_full[raw_of(w)], 16)

            def load_ada(s, b, i=None):
                old = A0[s] + b - 2
                if old in DIRECT_UNITS:
                    sp.wait_ge(ada_direct, taken_by_pe(old) + 1)
                else:
                    sp.wait_ge(ada_ready, at(taken_by_dve(old) + 1, i, 2))
                n = b if i is None else i * 2 + b
                slot = (A0[s] + b) % 2
                sp.dma_start(ada[:, slot, :, :], ada_source(s, n)).then_inc(ada_full[slot], 16)

            sp.dma_start(ident, consts[:, K_IDENT:K_IDENT + P]).then_inc(c_full, 16)
            sp.dma_start(c_rows[0:8, :], a["c"][0].rearrange("(r c) -> r c", c=P)).then_inc(c_full, 16)
            sp.dma_start(c_rows[8:16, :], a["c_2"][0].rearrange("(r c) -> r c", c=P)).then_inc(c_full, 16)
            for r in range(8):
                if r == 2:
                    sp.dma_start(x_in[:, :, :], a["x"][0].rearrange("(t p) d -> p t d", p=P)).then_inc(x_full, 16)
                src = ada_1[:, :, CW * r:CW * (r + 1)]
                if r in PRO_PE:
                    n = PRO_PE.index(r)
                    dst = raw[:, n, :].rearrange("p (k n) -> p k n", k=KD)
                    sp.dma_start(dst, src).then_inc(raw_full[n], 16)
                else:
                    n = PRO_DVE.index(r)
                    if n >= 2:
                        sp.wait_ge(ada_ready, n - 1)
                    sp.dma_start(ada[:, n % 2, :, :], src).then_inc(ada_full[n % 2], 16)

            for s, kind in enumerate(KINDS):
                if kind in HEADS:
                    after = ADA_AFTER[kind]
                    b = 0
                    for m in range(NUNITS[kind]):
                        load(W0[s] + m, *unit_source(s, m))
                        while b < N_ADA[s] and (m >= 2 * b if b < 2 else after[b - 2] + NBUF <= m) and not (
                                kind == "fox" and b >= 9 and m < NUNITS[kind] - 1):
                            load_ada(s, b)
                            b += 1
                    late = list(range(b, N_ADA[s]))
                else:
                    up, down = ffn_weights(s)
                    up_v = all_rows(up)
                    down_v = down.rearrange("(k p) n -> p k n", p=P)
                    base = W0[s]
                    load(base, up_v[:, :, 0:CW], KD)
                    load(base + 1, up_v[:, :, FF:FF + CW], KD)
                    for b in late:
                        load_ada(s - 1, b)
                    for b in range(2 if N_ADA[s] else 0):
                        load_ada(s, b)
                    with sp.Fori(0, PAIRS) as i:
                        for e in range(2):
                            u = base + 2 + 3 * e
                            col = i * (2 * CW) + CW * (e + 1)
                            load(u, up_v[:, :, bass.ds(col, CW)], KD, i)
                            load(u + 1, up_v[:, :, bass.ds(col + FF, CW)], KD, i)
                            if N_ADA[s]:
                                load_ada(s, e + 2, i)
                            load(u + 2, down_v[:, bass.ds(i * 4 + 2 * e, 2), :], 2, i)
                    load(base + 3 * FIT - 1, down_v[:, 2 * FIT - 2:2 * FIT, :], 2)
                    late = []

            for t in range(2):
                sp.wait_ge(y_ready, 2 * (t + 1))
                sp.dma_start(out[0, P * t:P * (t + 1), :], V[:, t, :]).then_inc(stored, 16)
            sp.wait_ge(stored, 32)

        @block.gpsimd
        def _(pool):
            pool.dma_start(kon[:, P:K_END], consts[:, P:K_END]).then_inc(small_full, 16)
            pool.dma_start(tables, buckets).then_inc(small_full, 16)
            pool.wait_ge(ones_set, 1)
            pool.dma_start(rel[0:32, 0:8], a["rel_bias"]).then_inc(small_full, 16)
            pool.dma_start(rel[0:32, 8:24], a["rel_bias_2"]).then_inc(small_full, 16)
            pool.dma_start(f_w[:, :, :], all_rows(a["fox_w_in_2"][0])[:, :, 3 * D:3 * D + 16]).then_inc(small_full, 16)
            pool.dma_start(pool_w[:, :, :], a["pool_w"][0].rearrange("g c d -> c g d")).then_inc(small_full, 16)
            over_partitions = lambda ap: bass.AP(tensor=ap.tensor, offset=ap.offset, ap=[[0, P], [1, 16]])
            pool.dma_start(sink[:, :], over_partitions(a["swa_sink_2"][0:1, :])).then_inc(small_full, 16)
            for t in range(2):
                pool.dma_start(fb[:, t, :], over_partitions(a["fox_b_f_2"][0:1, :])).then_inc(small_full, 16)

            def by_distance(n, heads):
                src = bass.AP(tensor=scratch.tensor, offset=scratch.offset + n * 16 * 384,
                              ap=[[1, P], [384, heads], [1, T]])
                pool.dma_start(TB[:, 0:heads, :], src).then_inc(bias_in, 16)

            pool.wait_ge(bias_rows, 1)
            for n in range(2):
                heads = (8, 16)[n]
                pool.dma_start(scratch[n, 0:heads, :], table_rows[0:heads, n, :]).then_inc(bias_out, 16)
            pool.wait_ge(bias_out, 32)
            pool.wait_ge(cols_done, 2)
            by_distance(0, 8)
            pool.wait_ge(merged, 4)
            by_distance(1, 16)
            pool.wait_ge(nft_ready, 1)
            pool.dma_start(scratch_f[:, :], nFT[:, :]).then_inc(forget_out, 16)
            pool.wait_ge(forget_out, 16)
            src = bass.AP(tensor=scratch_f.tensor, offset=scratch_f.offset, ap=[[0, P], [1, 16 * T]])
            pool.dma_start(TB[:, :, :].rearrange("p a b -> p (a b)"), src).then_inc(bias_in, 16)

        @block.scalar
        def _(act):
            def split_hi(w, i=None):
                act.wait_ge(raw_full[raw_of(w)], at(16 * ((w + PRO) // NBUF + 1), i, 32))
                if w >= NBUF:
                    act.wait_ge(unit_done, at(w - NBUF + 1, i, 6))
                nc.scalar.activation(hi[:, split_of(w), :], raw[:, raw_of(w), :], ACT.Copy).then_inc(hi_ready, 1)

            next_hi = 0

            def split_through(s, u):
                nonlocal next_hi
                while next_hi <= W0[s] + u and next_hi < W0[-1]:
                    split_hi(next_hi)
                    next_hi += 1

            def norm_stats(s):
                nc.scalar.activation(warm[:, :], eps[:, :], ACT.Sqrt)
                for k in range(KD):
                    act.wait_ge(x_ready, KD * s + k + 1 + (k + 1) % 2 * (s == 0))
                    if k >= 4:
                        act.wait_ge(sq_used, (KD - 1) * s + k - 3)
                    nc.scalar.activation(sq[:, k % 4, :], xT[:, k, :], ACT.Square).then_inc(sq_ready, 1)
                act.wait_ge(stats_done, s + 1)
                nc.scalar.activation(std[:, 0, 0:T], S[:, 0:T], ACT.Sqrt, bias=eps[:, 0:1],
                                     scale=1.0 / D).then_inc(std_ready, 1)

            def norm_apply(s):
                for k in range(KD):
                    act.wait_ge(t_ready, KD * s + k + 1)
                    nc.scalar.activation(h_hi[:, k, :], tn[:, k % 4, :], ACT.Identity,
                                         bias=modc[:, s % 2, k:k + 1]).then_inc(hhi_ready, 1)

            def ffn_step(s, j, i=None):
                base, f = W0[s], FFN_NO[s]
                n = base + 3 * j
                gate, up = (n - 1, n) if j else (n, n + 1)
                if KINDS[s] == "conv":
                    def convolve_last(q):
                        tile = 2 * j + q % 2 + (FF // P) * (q // 2)
                        col = lambda c: cols[:, c + tile:c + tile + 1] if i is None else cols[:, bass.ds(i * 4 + c + tile, 1)]
                        nc.scalar.activation(cv[:, q, :], G[q // 2][:, T * (q % 2):T * (q % 2 + 1)], ACT.Identity,
                                             bias=col(C_CONVB), scale=col(C_CONVW[2])).then_inc(cv_ready, 1)

                    if j:
                        act.wait_ge(mul_done, at(j, i, 2))
                    act.wait_ge(unit_done, at(gate + 1, i, 6))
                    convolve_last(0)
                    convolve_last(1)
                    split_hi(n + 2, i)
                    act.wait_ge(conv_done, at(4 * j + 2, i, 8))
                    nc.scalar.activation(sil[:, j % 2, :, :], cv[:, 0:2, :], ACT.Silu).then_inc(silu_ready, 1)
                    act.wait_ge(unit_done, at(up + 1, i, 6))
                    convolve_last(2)
                    convolve_last(3)
                else:
                    split_hi(n + 2, i)
                    act.wait_ge(unit_done, at(gate + 1, i, 6))
                    nc.scalar.activation(sil[:, j % 2, :, :].rearrange("p a b -> p (a b)"), G[0][:, :],
                                         ACT.Silu).then_inc(silu_ready, 1)
                if n + 3 < W0[-1]:
                    split_hi(n + 3, i)
                    split_hi(n + 4, i)

            def q_square(s, u):
                q = QK_UNITS[KINDS[s]].index(u)
                act.wait_ge(unit_done, W0[s] + u + 1)
                if q >= 2:
                    act.wait_ge(qs_done, QK0[s] + q - 1)
                nc.scalar.activation(sq[:, 2 * (q % 2):2 * (q % 2) + 2, :].rearrange("p a b -> p (a b)"),
                                     bank_of(s, u)[:, :], ACT.Square).then_inc(qsq_ready, 1)

            def q_std(s, q):
                act.wait_ge(qs_done, QK0[s] + q + 1)
                if q >= 2:
                    act.wait_ge(qk_ready, QK0[s] + q - 1)
                nc.scalar.activation(hstd[:, q % 2, :], A[1][:, 0:8], ACT.Sqrt, bias=eps[:, 0:1],
                                     scale=1.0 / HD).then_inc(qstd_ready, 1)

            def q_copy(s, u):
                q = QK_UNITS[KINDS[s]].index(u)
                act.wait_ge(qb_done, QK0[s] + q + 1)
                if q >= 2:
                    act.wait_ge(qk_ready, QK0[s] + q - 1)
                nc.scalar.activation(std[:, q % 2, :], S[:, :], ACT.Copy).then_inc(qc_ready, 1)

            def v_copy(s, v):
                u = V_UNITS[KINDS[s]][v]
                act.wait_ge(unit_done, W0[s] + u + 1)
                if s == 0 and v == 0:
                    act.wait_ge(bias_out, 32)
                nc.scalar.activation(V[:, :, CW * v:CW * (v + 1)], G[u % 2][:, :].rearrange("p (a b) -> p a b", a=2),
                                     ACT.Copy).then_inc(v_ready, 1)

            def exps(s, h):
                n = HEAD0[s] + h
                st, pr = stat[:, n % 3, :], P_of[n % 3]
                act.wait_ge(am_done, n + 1)
                nc.scalar.activation(pr[:, 0:P], pr[:, 0:P], ACT.Exp, bias=st[:, 2:3], accum_out=st[:, 4:5])
                ins = nc.scalar.activation(pr[:, P:384], pr[:, P:384], ACT.Exp, bias=st[:, 3:4], accum_out=st[:, 5:6])
                if KINDS[s] == "swa":
                    ins = nc.scalar.activation(st[:, 6:8], st[:, 6:8], ACT.Exp)
                ins.then_inc(exp_done, 1)

            def pt_copy(s, h):
                n = HEAD0[s] + h
                act.wait_ge(tr_done, n + 1)
                if n >= 2:
                    act.wait_ge(pv_done, n - 1)
                dst = PT_of[n % 2].rearrange("p (a b) -> p a b", a=3)
                if KINDS[s] != "fox":
                    dst = dst[:, :, ::-1]
                nc.scalar.activation(dst, A[2][:, 0:384].rearrange("p (a b) -> p a b", a=3),
                                     ACT.Copy).then_inc(ptc_done, 1)

            def out_hi(s, pair):
                n = HEAD0[s] // 2 + pair
                act.wait_ge(pv_done, 2 * n + 2)
                nc.scalar.activation(o_hi[:, pair, :], (A[3], S)[n % 2][:, 0:T], ACT.Copy).then_inc(ohi_done, 1)

            def attention_step(s, t):
                nh = HEADS[KINDS[s]]
                if t < nh:
                    exps(s, t)
                if 0 <= t - 2 < nh:
                    pt_copy(s, t - 2)
                if 0 <= t - 4 < nh and (t - 4) % 2:
                    out_hi(s, (t - 4) // 2)

            act.wait_ge(c_turned, 1)
            nc.scalar.activation(c_act[:, :], S[:, 0:16], ACT.Silu).then_inc(c_done, 1)
            act.wait_ge(rows_clear, 1)
            r128 = lambda ap: ap.rearrange("(r c) -> r c", c=P)
            for tile, first, src in [
                (0, 0, r128(a["ada_b"][0])),
                (0, 64, r128(a["norm1_g"][0])), (0, 72, r128(a["norm2_g"][0])),
                (0, 80, a["norm_g_2"].rearrange("l s (r c) -> (l s r) c", c=P)),
                (1, 0, r128(a["ada_b_2"][0])), (1, 72, r128(a["conv_b"][0])), (1, 116, r128(a["pool_scale"][0])),
                (2, 0, r128(a["ada_b_2"][1])), (2, 72, r128(a["conv_w"][0, 0])),
                (3, 0, r128(a["conv_w"][0, 1])), (3, 44, r128(a["conv_w"][0, 2])),
            ]:
                act.dma_start(rows[first:first + src.shape[0], tile, :], src).then_inc(rows_full, 16)
            for n, name in enumerate(["q_norm_g", "k_norm_g", "swa_q_g_2", "swa_k_g_2", "fox_q_g_2", "fox_k_g_2"]):
                for c in range(2):
                    act.dma_start(rows[120 + n:121 + n, 1, HD * c:HD * (c + 1)], a[name][0:1, :]).then_inc(rows_full, 16)
            act.wait_ge(small_full, SMALL_LOADED)
            nc.scalar.activation(f_hi[:, :, :], f_w[:, :, :], ACT.Copy).then_inc(f_hi_done, 1)

            for s, kind in enumerate(KINDS):
                base = W0[s]
                norm_stats(s)
                split_through(0, 1)
                norm_apply(s)
                if kind in ("conv", "ffn"):
                    turns = PAIRS - (s == len(KINDS) - 1)
                    ffn_step(s, 0)
                    with act.Fori(0, turns) as i:
                        ffn_step(s, 1, i)
                        ffn_step(s, 2, i)
                    for j in range(1 + 2 * turns, FIT):
                        ffn_step(s, j)
                    next_hi = W0[s + 1] + 2
                elif kind == "moba":
                    for u in range(4):
                        split_through(s, u + 2)
                        if u:
                            q_std(s, u - 1)
                        if u >= 2:
                            q_copy(s, u - 2)
                        q_square(s, u)
                    split_through(s, 6)
                    q_std(s, 3)
                    q_copy(s, 2)
                    v_copy(s, 0)
                    q_copy(s, 3)
                    for t in range(HEADS[kind] + 4):
                        attention_step(s, t)
                        if t == 2:
                            split_through(s, 7)
                            v_copy(s, 1)
                        if t in (4, 6):
                            split_through(s, 8 + (t - 4) // 2)
                            i = (t - 4) // 2
                            act.wait_ge(unit_done, base + 7 + i)
                            nc.scalar.activation(V[:, i, 512:1024], G[i % 2][:, :], ACT.Copy).then_inc(p_ready, 1)
                    for r in range(8):
                        split_through(s, 10 + r)
                        act.wait_ge(unit_done, base + 9 + r)
                        dst = (TB[:, 8 + 2 * r:10 + 2 * r, :] if r < 4 else
                               (QT if r < 6 else KT)[:, 4 + 2 * (r % 2):6 + 2 * (r % 2), :])
                        nc.scalar.activation(dst.rearrange("p a b -> p (a b)"), G[r % 2][:, :],
                                             ACT.Sigmoid).then_inc(sig_ready, 1)
                        if r == 5:
                            for g in range(4):
                                act.wait_ge(pw_done, g // 2 * 2 + 2)
                                nc.scalar.activation(sq[:, g, :], A[g // 2][:, T * (g % 2):T * (g % 2 + 1)], ACT.Copy,
                                                     scale=cols[:, C_PSCALE + g:C_PSCALE + g + 1]).then_inc(ps_ready, 1)
                    split_through(s, NUNITS[kind] + 1)
                elif kind == "swa":
                    split_through(s, 2)
                    q_square(s, 0)
                    split_through(s, 3)
                    q_std(s, 0)
                    v_copy(s, 0)
                    split_through(s, 4)
                    q_copy(s, 0)
                    q_square(s, 2)
                    for q, u in enumerate(QK_UNITS[kind]):
                        if u >= 3:
                            split_through(s, u + 2)
                            q_std(s, q - 1)
                            if u >= 4:
                                q_copy(s, u - 2)
                            if u == 5:
                                for n in range(2):
                                    act.wait_ge(dup_done, n + 1)
                                    nc.scalar.activation(KT[:, 4 + 2 * n:6 + 2 * n, :].rearrange("p a b -> p (a b)"),
                                                         A[2 * n][:, :], ACT.Copy).then_inc(dup_ready, 1)
                            q_square(s, u)
                    q_copy(s, 4)
                    q_std(s, 4)
                    q_copy(s, 5)
                    for t in range(HEADS[kind] + 4):
                        attention_step(s, t)
                        if t == 13:
                            split_through(s, 8)
                    split_through(s, NUNITS[kind] + 1)
                else:
                    for u in range(8):
                        split_through(s, u + 2)
                        if u:
                            q_std(s, u - 1)
                        if u >= 2:
                            q_copy(s, u - 2)
                        if u == 1:
                            act.wait_ge(fz_ready, 2)
                            nc.scalar.activation(fz[:, 2, :], fz[:, 1, :], ACT.Exp).then_inc(f_exp, 1)
                            act.wait_ge(f_exp, 1)
                            nc.scalar.activation(fz[:, 3, :], fz[:, 2, :], ACT.Ln, bias=ones[:, 0:1]).then_inc(f_ln, 1)
                        q_square(s, u)
                    split_through(s, 10)
                    q_std(s, 7)
                    q_copy(s, 6)
                    v_copy(s, 0)
                    q_copy(s, 7)
                    for t in range(HEADS[kind] + 4):
                        attention_step(s, t)
                        if t in (3, 7, 11):
                            v = (t - 3) // 4 + 1
                            split_through(s, 10 + v)
                            v_copy(s, v)
                    split_through(s, NUNITS[kind] + 1)

        @block.vector
        def _(dve):
            pool_steps = 0

            def split_lo(w, i=None):
                dve.wait_ge(hi_ready, at(w + 1, i, 6))
                nc.vector.tensor_tensor(lo[:, split_of(w), :], raw[:, raw_of(w), :],
                                        hi[:, split_of(w), :].bitcast(F32), ALU.subtract).then_inc(lo_ready, 1)

            def ada_unit(s, b, i=None):
                ada_sum_of(A0[s] + b, 0 if s == 0 else 8, i)

            def ada_sum_of(n, c, i=None):
                slot, m = n % 2, taken_by_dve(n)
                dve.wait_ge(ada_full[slot], at(16 * (n // 2 + 1), i, 16))
                if m >= 2:
                    dve.wait_ge(ada_used, at(m - 1, i, 2))
                acc = ada_sum[:, m % 2, :]
                nc.vector.tensor_scalar(acc, ada[:, slot, 0, :], c_act[:, c:c + 1], None, ALU.mult).then_inc(ada_step, 1)
                for k in range(1, KD):
                    dve.wait_ge(ada_step, at(7 * m + k, i, 14))
                    nc.vector.scalar_tensor_tensor(acc, in0=ada[:, slot, k, :], scalar=c_act[:, c + k:c + k + 1],
                                                   in1=acc, op0=ALU.mult, op1=ALU.add
                                                   ).then_inc(ada_step if k < KD - 1 else ada_ready, 1)

            next_lo = 0

            def split_through(s, u):
                nonlocal next_lo
                while next_lo <= W0[s] + u:
                    split_lo(next_lo)
                    for b, m in enumerate(ADA_AFTER[KINDS[s]]):
                        if m == next_lo - W0[s] and b not in DIRECT[KINDS[s]]:
                            ada_unit(s, b)
                    next_lo += 1

            def mod_columns(s):
                par = s % 2
                if s == 0:
                    dve.wait_ge(pro_done, PRO)
                    dve.wait_ge(ada_used, len(PRO_DVE))
                    nc.vector.tensor_tensor(modc[:, 0, 0:16], M[:, 0:16], cols[:, 0:16], ALU.add).then_inc(mod_ready, 1)
                    dve.wait_ge(mod_ready, 1)
                    gain = C_N1
                elif s == 1:
                    dve.wait_ge(ada_used, taken_by_dve(A0[1]))
                    dve.wait_ge(ada_direct, taken_by_pe(A0[1]))
                    nc.vector.tensor_tensor(gate0[:, :], M[:, 0:8], cols[:, 16:24], ALU.add)
                    nc.vector.tensor_tensor(modc[:, 1, :], M[:, 8:32], cols[:, 24:48], ALU.add).then_inc(mod_ready, 1)
                    dve.wait_ge(mod_ready, 3)
                    gain = C_N2
                else:
                    l, stage = divmod(s - 2, 3)
                    first = C_ADAB2[l] + 24 * stage
                    dve.wait_ge(ada_used, taken_by_dve(A0[s]))
                    dve.wait_ge(ada_direct, taken_by_pe(A0[s]))
                    nc.vector.tensor_tensor(modc[:, par, :], M[:, 0:24], cols[:, first:first + 24], ALU.add).then_inc(mod_ready, 1)
                    dve.wait_ge(mod_ready, 2 * s + 1)
                    gain = C_NG2 + 8 * (s - 2)
                if s >= 2 and KINDS[s] == "ffn":
                    nc.vector.tensor_scalar(modc[:, par, 16:24], modc[:, par, 16:24], 0.5, None, ALU.mult)
                nc.vector.scalar_tensor_tensor(acol[:, par, :], in0=modc[:, par, 8:16], scalar=1.0,
                                               in1=cols[:, gain:gain + 8], op0=ALU.add, op1=ALU.mult).then_inc(mod_ready, 1)
                dve.wait_ge(mod_ready, 2 * s + 2)

            def norm_stats(s):
                dve.wait_ge(std_ready, s + 1)
                nc.vector.reciprocal(std[:, 1, 0:T], std[:, 0, 0:T]).then_inc(rstd_ready, 1)
                dve.wait_ge(rstd_ready, s + 1)

            def norm_apply(s):
                par = s % 2
                for k in range(KD + 1):
                    if k < KD:
                        nc.vector.scalar_tensor_tensor(tn[:, k % 4, :], in0=xT[:, k, :], scalar=acol[:, par, k:k + 1],
                                                       in1=std[:, 1, 0:T], op0=ALU.mult, op1=ALU.mult).then_inc(t_ready, 1)
                    if k:
                        dve.wait_ge(hhi_ready, KD * s + k)
                        nc.vector.scalar_tensor_tensor(h_lo[:, k - 1, :], in0=tn[:, (k - 1) % 4, :],
                                                       scalar=modc[:, par, k - 1:k], in1=h_hi[:, k - 1, :].bitcast(F32),
                                                       op0=ALU.add, op1=ALU.subtract).then_inc(h_ready, 1)

            def residual(s, n, psum):
                gate = gate0[:, n:n + 1] if s == 0 else modc[:, s % 2, 16 + n:17 + n]
                nc.vector.scalar_tensor_tensor(xT[:, n, :], in0=psum, scalar=gate, in1=xT[:, n, :],
                                               op0=ALU.mult, op1=ALU.add).then_inc(x_ready, 1)

            def ffn_step(s, j, i=None):
                n, f = W0[s] + 3 * j, FFN_NO[s]
                up = n if j else n + 1
                done = FIT * f + j + 1
                if KINDS[s] == "conv":
                    def taps(q0):
                        dve.wait_ge(cv_ready, at(4 * j + q0 + 2, i, 8))
                        for back, c0, ready in ((1, C_CONVW[1], tap_done), (2, C_CONVW[0], conv_done)):
                            for q in (q0, q0 + 1):
                                tile = 2 * j + q % 2 + (FF // P) * (q // 2)
                                col = cols[:, c0 + tile:c0 + tile + 1] if i is None else cols[:, bass.ds(i * 4 + c0 + tile, 1)]
                                if back == 2:
                                    dve.wait_ge(tap_done, at(4 * j + q + 1, i, 8))
                                u = G[q // 2][:, T * (q % 2):T * (q % 2 + 1)]
                                nc.vector.scalar_tensor_tensor(cv[:, q, back:T], in0=u[:, 0:T - back], scalar=col,
                                                               in1=cv[:, q, back:T], op0=ALU.mult, op1=ALU.add
                                                               ).then_inc(ready, 1)

                    taps(0)
                    split_lo(n + 2, i)
                    taps(2)
                    dve.wait_ge(silu_ready, at(done, i, 2))
                    dve.wait_ge(conv_done, at(4 * j + 4, i, 8))
                    nc.vector.tensor_tensor(prod, sil[:, j % 2, :, :], cv[:, 2:4, :], ALU.mult).then_inc(mul_done, 1)
                else:
                    split_lo(n + 2, i)
                    dve.wait_ge(silu_ready, at(done, i, 2))
                    dve.wait_ge(unit_done, at(up + 1, i, 6))
                    nc.vector.tensor_tensor(prod.rearrange("p a b -> p (a b)"),
                                            sil[:, j % 2, :, :].rearrange("p a b -> p (a b)"), G[1][:, :],
                                            ALU.mult).then_inc(mul_done, 1)
                dve.wait_ge(mul_done, at(done, i, 2))
                nc.vector.tensor_copy(hid_hi[:, j % 2, :, :], prod).then_inc(hid_hi_done, 1)
                dve.wait_ge(hid_hi_done, at(done, i, 2))
                nc.vector.tensor_tensor(hid_lo[:, j % 2, :, :], prod, hid_hi[:, j % 2, :, :].bitcast(F32),
                                        ALU.subtract).then_inc(hid_ready, 1)
                if n + 3 < W0[-1]:
                    split_lo(n + 3, i)
                if N_ADA[s]:
                    ada_unit(s, j + 1, i)
                if n + 4 < W0[-1]:
                    split_lo(n + 4, i)

            def q_reciprocal(s, u):
                q = QK_UNITS[KINDS[s]].index(u)
                dve.wait_ge(qstd_ready, QK0[s] + q + 1)
                nc.vector.reciprocal(hstd[:, q % 2, :], hstd[:, q % 2, :]).then_inc(qrs_ready, 1)

            def q_norm(s, u):
                kind = KINDS[s]
                q = QK_UNITS[kind].index(u)
                dve.wait_ge(qc_ready, QK0[s] + q + 1)
                is_q, n = {"moba": (u < 2, u % 2), "swa": (u >= 2, u - 2 if u >= 2 else 0),
                           "fox": (u % 2 == 0, u // 2)}[kind]
                gain = C_GAIN + {"moba": 0, "swa": 2, "fox": 4}[kind] + (0 if is_q else 1)
                dst = (QT if is_q else KT)[:, 2 * n:2 * n + 2, :]
                split4 = lambda ap: ap.rearrange("p (a b) -> p a b", b=P)
                dst = split4(dst.rearrange("p a b -> p (a b)"))
                if is_q and kind != "fox":
                    dst = dst[:, :, ::-1]
                nc.vector.scalar_tensor_tensor(dst, in0=split4(bank_of(s, u)[:, :]), scalar=cols[:, gain:gain + 1],
                                               in1=split4(std[:, q % 2, :]), op0=ALU.mult, op1=ALU.mult).then_inc(qk_ready, 1)

            def max_of(s, h):
                kind = KINDS[s]
                n = HEAD0[s] + h
                st, pr, L = stat[:, n % 3, :], P_of[n % 3], A[n % 2]
                first = 0.0
                b0, b1 = TB[:, h, P:2 * P], TB[:, h, :]
                if kind == "fox":
                    f0, f1 = tn[:, 0, 0:P], tn[:, 1, :]
                    if h % 2:
                        f0, f1 = tn[:, 2, 0:P], tn[:, 3, :]
                    nc.vector.scalar_tensor_tensor(f0, in0=TB[:, h, 0:P], scalar=Fq[:, 0, h:h + 1], in1=mask[:, P:2 * P],
                                                   op0=ALU.add, op1=ALU.add)
                    nc.vector.scalar_tensor_tensor(f1, in0=TB[:, h, :], scalar=Fq[:, 1, h:h + 1], in1=mask,
                                                   op0=ALU.add, op1=ALU.add).then_inc(bias_ready, 1)
                    b0, b1 = f0, f1
                    dve.wait_ge(bias_ready, h + 1)
                least = sink[:, h:h + 1] if kind == "swa" else LOWEST
                dve.wait_ge(qk_done, n + 1)
                if n >= 3:
                    dve.wait_ge(tr_done, n - 2)
                nc.vector.tensor_tensor_reduce(pr[:, 0:P], L[:, 0:P], b0, 1.0, least, ALU.add, ALU.max, st[:, 0:1])
                nc.vector.tensor_tensor_reduce(pr[:, P:384], L[:, P:384], b1, 1.0, least, ALU.add, ALU.max,
                                               st[:, 1:2]).then_inc(max_done, 1)
                dve.wait_ge(max_done, n + 1)
                ins = nc.vector.tensor_scalar(st[:, 2:4], st[:, 0:2], -1.0, None, ALU.mult)
                if kind == "swa":
                    ins.then_inc(neg_done, 1)
                    dve.wait_ge(neg_done, h + 1)
                    ins = nc.vector.tensor_scalar(st[:, 6:8], st[:, 2:4], sink[:, h:h + 1], None, ALU.add)
                ins.then_inc(am_done, 1)

            def normalise(s, h):
                n = HEAD0[s] + h
                st, pr = stat[:, n % 3, :], P_of[n % 3]
                dve.wait_ge(exp_done, n + 1)
                if KINDS[s] == "swa":
                    nc.vector.tensor_tensor(st[:, 4:6], st[:, 4:6], st[:, 6:8], ALU.add).then_inc(den_ready, 1)
                    dve.wait_ge(den_ready, HEAD0[s] + 2 * h + 1)
                nc.vector.reciprocal(st[:, 4:6], st[:, 4:6]).then_inc(den_ready, 1)
                dve.wait_ge(den_ready, n + 1 + (h + 1 if KINDS[s] == "swa" else 16 if KINDS[s] == "fox" else 0))
                nc.vector.tensor_scalar(pr[:, 0:P], pr[:, 0:P], st[:, 4:5], None, ALU.mult)
                nc.vector.tensor_scalar(pr[:, P:384], pr[:, P:384], st[:, 5:6], None, ALU.mult).then_inc(nm_done, 1)

            def out_lo(s, pair):
                n = HEAD0[s] // 2 + pair
                dve.wait_ge(ohi_done, n + 1)
                nc.vector.tensor_tensor(o_lo[:, pair, :], (A[3], S)[n % 2][:, 0:T], o_hi[:, pair, :].bitcast(F32),
                                        ALU.subtract).then_inc(olo_done, 1)

            def attention_step(s, t):
                nh = HEADS[KINDS[s]]
                if t < nh:
                    max_of(s, t)
                if 0 <= t - 1 < nh:
                    normalise(s, t - 1)
                if 0 <= t - 5 < nh and (t - 5) % 2:
                    out_lo(s, (t - 5) // 2)

            def out_units(s):
                kind = KINDS[s]
                for o in range(4):
                    u = OUT_UNITS[kind] + o
                    split_through(s, u + 1)
                    dve.wait_ge(unit_done, W0[s] + u + 1)
                    for n in range(2):
                        residual(s, 2 * o + n, G[o % 2][:, T * n:T * (n + 1)])
                split_through(s, NUNITS[kind] + 1)

            def step(ins):
                nonlocal pool_steps
                pool_steps += 1
                ins.then_inc(pool_step, 1)
                dve.wait_ge(pool_step, pool_steps)

            def pool_branch(g):
                w = WINDOWS[g]
                src = V[:, g // 2, 512 + T * (g % 2):512 + T * (g % 2 + 1)]
                have, shift = src, 1
                n = 0
                while shift < w:
                    nxt = sq[:, n % 2, :]
                    nc.vector.tensor_copy(nxt[:, 0:shift], have[:, 0:shift])
                    step(nc.vector.tensor_tensor(nxt[:, shift:T], have[:, shift:T], have[:, 0:T - shift], ALU.add))
                    have, shift, n = nxt, 2 * shift, n + 1
                mean = sq[:, 2, 0:16]
                step(nc.vector.tensor_tensor(mean, have[:, 0:16], kon[:, K_INV + 16 * g:K_INV + 16 * (g + 1)], ALU.mult))
                dst = std[:, g // 2, T * (g % 2):T * (g % 2 + 1)]
                nc.vector.tensor_tensor(dst[:, 0:16], mean, src[:, 0:16], ALU.subtract)
                nc.vector.scalar_tensor_tensor(dst[:, 16:T], in0=have[:, 16:T], scalar=1.0 / w, in1=src[:, 16:T],
                                               op0=ALU.mult, op1=ALU.subtract).then_inc(pool_ready, 1)

            def merge(half, splits):
                base = W0[0]
                flat = lambda ap: ap.rearrange("p a b -> p (a b)")
                pair = (2 * half, 2 * half + 1)
                ma = lambda n: work[:, 1024 * (n % 2):1024 * (n % 2) + 512]
                mb = lambda n: work[:, 1024 * (n % 2) + 512:1024 * (n % 2 + 1)]
                dve.wait_ge(unit_done, base + 17 + 2 * half)
                if half:
                    dve.wait_ge(merged, 2)
                for n in pair:
                    nc.vector.tensor_tensor(ma(n), A[n % 2][:, :], flat(TB[:, 8 + 2 * n:10 + 2 * n, :]),
                                            ALU.mult).then_inc(merge_a, 1)
                split_through(0, splits)
                dve.wait_ge(unit_done, base + 18 + 2 * half)
                for n in pair:
                    gate_p = (QT if n < 2 else KT)[:, 4 + 2 * (n % 2):6 + 2 * (n % 2), :]
                    nc.vector.tensor_tensor(mb(n), A[2 + n % 2][:, :], flat(gate_p), ALU.mult).then_inc(merge_b, 1)
                for n in pair:
                    dve.wait_ge(merge_b, n + 1)
                    nc.vector.tensor_tensor(ma(n), ma(n), mb(n), ALU.add).then_inc(merge_s, 1)
                for n in pair:
                    dve.wait_ge(merge_s, n + 1)
                    nc.vector.tensor_copy(flat(h_hi[:, 2 * n:2 * n + 2, :]), ma(n)).then_inc(merge_hi, 1)
                for n in pair:
                    dve.wait_ge(merge_hi, n + 1)
                    nc.vector.tensor_tensor(flat(h_lo[:, 2 * n:2 * n + 2, :]), ma(n),
                                            flat(h_hi[:, 2 * n:2 * n + 2, :]).bitcast(F32), ALU.subtract).then_inc(merged, 1)

            nc.vector.memset(rows[:, :, :], 0.0).then_inc(rows_clear, 1)
            nc.vector.memset(ones[:, :], 1.0)
            nc.vector.memset(zeros[:, :], 0.0)
            nc.vector.memset(eps[:, :], EPS)
            nc.vector.memset(rel[:, :], 1.0).then_inc(ones_set, 1)
            dve.wait_ge(c_done, 1)
            ada_sum_of(0, 0)
            for b in range(4):
                dve.wait_ge(x_turned, b + 1)
                nc.vector.tensor_copy(xT[:, 2 * b:2 * b + 2, :].rearrange("p a b -> p (a b)"), A[b][:, :]).then_inc(x_ready, 2)
            ada_sum_of(1, 0)
            dve.wait_ge(rows_turned, 1)
            nc.vector.tensor_copy(cols[:, :], G[0][:, :]).then_inc(cols_done, 1)
            dve.wait_ge(cols_done, 1)
            nc.vector.tensor_scalar(cols[:, C_GAIN:C_GAIN + 6:2], cols[:, C_GAIN:C_GAIN + 6:2], HD ** -0.5, None,
                                    ALU.mult).then_inc(cols_done, 1)
            ada_sum_of(2, 0)
            for n in range(2):
                heads = (8, 16)[n]
                dve.wait_ge(bias_sum, n + 1)
                ins = nc.vector.tensor_copy(table_rows[0:heads, n, :], G[n][0:heads, 0:384])
            ins.then_inc(bias_rows, 1)
            for n in range(3, len(PRO_DVE)):
                ada_sum_of(n, 0)
            dve.wait_ge(f_hi_done, 1)
            nc.vector.tensor_tensor(f_lo[:, :, :], f_w[:, :, :], f_hi[:, :, :].bitcast(F32), ALU.subtract).then_inc(f_lo_done, 1)
            for s, kind in enumerate(KINDS):
                base = W0[s]
                norm_stats(s)
                if s == 0:
                    mod_columns(0)
                    split_through(0, 0)
                norm_apply(s)
                if kind in ("conv", "ffn"):
                    turns = PAIRS - (s == len(KINDS) - 1)
                    if N_ADA[s]:
                        ada_unit(s, 0)
                    ffn_step(s, 0)
                    with dve.Fori(0, turns) as i:
                        ffn_step(s, 1, i)
                        ffn_step(s, 2, i)
                    for j in range(1 + 2 * turns, FIT):
                        ffn_step(s, j)
                    next_lo = W0[s + 1] + 2
                    for n in range(KD):
                        if n in (0, 2, 4):
                            dve.wait_ge(acc_done, 3 * FFN_NO[s] + n // 2 + 1)
                        if n == 6:
                            dve.wait_ge(unit_done, W0[s + 1])
                        residual(s, n, A[n // 2][:, T * (n % 2):T * (n % 2 + 1)])
                elif kind == "moba":
                    for u in range(4):
                        split_through(s, u + 2)
                        q_reciprocal(s, u)
                        if u:
                            q_norm(s, u - 1)
                    split_through(s, 5)
                    q_norm(s, 3)
                    dve.wait_ge(bias_in, 16)
                    for t in range(HEADS[kind] + 5):
                        attention_step(s, t)
                        if t == 1:
                            split_through(s, 6)
                        if t == 3:
                            split_through(s, 7)
                        if t in (5, 7):
                            split_through(s, 8 + (t - 5) // 2)
                    dve.wait_ge(p_ready, 2)
                    for r in range(8):
                        split_through(s, 10 + r)
                        if r < 4:
                            pool_branch(r)
                        if r == 6:
                            pm = sq[:, :, :].rearrange("p a b -> p (a b)")
                            ph = o_hi[:, 4:8, :].rearrange("p a b -> p (a b)")
                            pl = o_lo[:, 4:8, :].rearrange("p a b -> p (a b)")
                            dve.wait_ge(ps_ready, 4)
                            nc.vector.tensor_copy(ph, pm).then_inc(phi_done, 1)
                            dve.wait_ge(phi_done, 1)
                            nc.vector.tensor_tensor(pl, pm, ph.bitcast(F32), ALU.subtract).then_inc(pool_split, 1)
                    split_through(s, 18)
                    dve.wait_ge(sig_ready, 8)
                    merge(0, 19)
                    split_through(s, 20)
                    merge(1, 21)
                    mod_columns(1)
                    out_units(s)
                elif kind == "swa":
                    for q, u in enumerate(QK_UNITS[kind]):
                        split_through(s, u + 2)
                        q_reciprocal(s, u)
                        if q:
                            q_norm(s, QK_UNITS[kind][q - 1])
                    q_norm(s, 5)
                    dve.wait_ge(bias_in, 32)
                    for t in range(HEADS[kind] + 5):
                        attention_step(s, t)
                        if t == 14:
                            split_through(s, 8)
                    out_units(s)
                else:
                    for u in range(8):
                        split_through(s, u + 2)
                        if u == 1:
                            dve.wait_ge(fl_done, 1)
                            nc.vector.tensor_tensor(fz[:, 0, :], A[0][:, 0:32], fb[:, :, :].rearrange("p a b -> p (a b)"),
                                                    ALU.add).then_inc(fz_ready, 1)
                            dve.wait_ge(fz_ready, 1)
                            nc.vector.scalar_tensor_tensor(fz[:, 1, :], in0=fz[:, 0, :], scalar=-1.0, in1=fz[:, 0, :],
                                                           op0=ALU.mult, op1=ALU.min).then_inc(fz_ready, 1)
                            dve.wait_ge(f_ln, 1)
                            nc.vector.scalar_tensor_tensor(fz[:, 4, :], in0=fz[:, 0, :], scalar=0.0, in1=fz[:, 3, :],
                                                           op0=ALU.min, op1=ALU.subtract).then_inc(lf_ready, 1)
                        if u == 3:
                            dve.wait_ge(cum_done, 1)
                            nc.vector.tensor_copy(Fq[:, :, :].rearrange("p a b -> p (a b)"), A[0][:, 64:96]).then_inc(fq_ready, 1)
                        if u == 5:
                            dve.wait_ge(ft_done, 1)
                            nc.vector.tensor_scalar(nFT[:, :], A[0][0:16, 128:128 + T], -1.0, None, ALU.mult).then_inc(nft_ready, 1)
                        q_reciprocal(s, u)
                        if u:
                            q_norm(s, u - 1)
                    split_through(s, 10)
                    q_norm(s, 7)
                    dve.wait_ge(bias_in, 48)
                    for t in range(HEADS[kind] + 5):
                        attention_step(s, t)
                        if t in (4, 8):
                            split_through(s, 11 + (t - 4) // 4)
                    out_units(s)
                if s + 1 < len(KINDS) and s > 0:
                    mod_columns(s + 1)
            for b in range(4):
                dve.wait_ge(y_turned, b + 1)
                nc.vector.tensor_copy(V[:, b // 2, 512 * (b % 2):512 * (b % 2 + 1)], (G[0], G[1], M, S)[b][:, :]).then_inc(y_ready, 1)

        @block.tensor
        def _(pe):
            mm = nc.tensor.matmul

            def product(outp, wh, wl, xh, xl, start, stop):
                mm(outp, wh, xh, start=start, stop=False, skip_group_check=True)
                mm(outp, wh, xl, start=False, stop=False, skip_group_check=True)
                return mm(outp, wl, xh, start=False, stop=stop, skip_group_check=True)

            def unit_of(w, tiles):
                s = split_of(w)
                cut = lambda ap: ap[:, s, :].rearrange("p (k n) -> p k n", k=tiles)
                return cut(hi), cut(lo)

            def half(w, bank, n, xh=h_hi, xl=h_lo, last=True):
                if n == 0:
                    pe.wait_ge(lo_ready, w + 1)
                wh, wl = unit_of(w, KD)
                for k in range(KD):
                    ins = product(bank[:, T * n:T * (n + 1)], wh[:, k, P * n:P * (n + 1)], wl[:, k, P * n:P * (n + 1)],
                                  xh[:, k, :], xl[:, k, :], k == 0, k == KD - 1)
                if n == 1:
                    ins.then_inc(unit_done, 1)

            def unit(w, bank, i=None, **kw):
                pe.wait_ge(lo_ready, at(w + 1, i, 6))
                wh, wl = unit_of(w, KD)
                for n in range(2):
                    for k in range(KD):
                        ins = product(bank[:, T * n:T * (n + 1)], wh[:, k, P * n:P * (n + 1)],
                                      wl[:, k, P * n:P * (n + 1)], h_hi[:, k, :], h_lo[:, k, :], k == 0, k == KD - 1)
                ins.then_inc(unit_done, 1)

            def first_unit(s, bank):
                w = W0[s]
                pe.wait_ge(lo_ready, w + 1)
                wh, wl = unit_of(w, KD)
                for k in range(KD):
                    pe.wait_ge(h_ready, KD * s + k + 1)
                    for n in range(2):
                        ins = product(bank[:, T * n:T * (n + 1)], wh[:, k, P * n:P * (n + 1)],
                                      wl[:, k, P * n:P * (n + 1)], h_hi[:, k, :], h_lo[:, k, :],
                                      k == 0 and n == 0, k == KD - 1)
                ins.then_inc(unit_done, 1)

            def v_half(w, bank, n):
                if n == 0:
                    pe.wait_ge(lo_ready, w + 1)
                wh, wl = unit_of(w, KD)
                for k in range(KD):
                    ins = product(bank[:, CW * n:CW * (n + 1)], h_hi[:, k, P * n:P * (n + 1)],
                                  h_lo[:, k, P * n:P * (n + 1)], wh[:, k, :], wl[:, k, :], k == 0, k == KD - 1)
                if n == 1:
                    ins.then_inc(unit_done, 1)

            def ada_reduce(s, b, i=None):
                if b == 0:
                    pe.wait_ge(mod_ready, 2 * s + 2)
                n = A0[s] + b
                if n in DIRECT_UNITS:
                    for quarter in range(4):
                        direct_quarter(s, b, quarter)
                else:
                    sum_partitions(n, 2 * b, i)

            def direct_quarter(s, b, quarter):
                n = A0[s] + b
                slot = n % 2
                if quarter == 0:
                    pe.wait_ge(ada_full[slot], 16 * (n // 2 + 1))
                c, half = divmod(quarter, 2)
                c0 = 0 if s == 0 else 8
                for k in range(4 * half, 4 * half + 4):
                    ins = mm(M[:, 2 * b + c:2 * b + c + 1], ada[:, slot, k, P * c:P * (c + 1)], c_act[:, c0 + k:c0 + k + 1],
                             start=k == 0, stop=k == KD - 1, skip_group_check=True)
                if quarter == 3:
                    ins.then_inc(ada_direct, 1)

            def times_c(w, col, c0):
                for c in range(2):
                    for k in range(KD):
                        ins = mm(M[:, col + c:col + c + 1], w[:, k, P * c:P * (c + 1)], c_act[:, c0 + k:c0 + k + 1],
                                 start=k == 0, stop=k == KD - 1)
                return ins

            def sum_partitions(n, col, i=None):
                m = taken_by_dve(n)
                pe.wait_ge(ada_ready, at(m + 1, i, 2))
                for c in range(2):
                    dst = M[:, col + c:col + c + 1] if i is None else M[:, bass.ds(i * 4 + col + c, 1)]
                    ins = mm(dst, ada_sum[:, m % 2, P * c:P * (c + 1)], ones[:, 0:1], start=True, stop=True)
                ins.then_inc(ada_used, 1)

            def norm(s):
                for k in range(KD):
                    pe.wait_ge(sq_ready, KD * s + k + 1)
                    ins = mm(S[:, 0:T], ones[:, :], sq[:, k % 4, :], start=k == 0, stop=k == KD - 1)
                    if k < KD - 1:
                        ins.then_inc(sq_used, 1)
                ins.then_inc(stats_done, 1)

            def down(w, step, order, i=None):
                pe.wait_ge(lo_ready, at(w + 1, i, 6))
                wh, wl = unit_of(w, 2)
                last = order == "tiles first"
                for n, k in ([(n, k) for n in range(KD) for k in range(2)] if last else
                             [(n, k) for k in range(2) for n in range(KD)]):
                    ins = product(A[n // 2][:, T * (n % 2):T * (n % 2 + 1)], wh[:, k, P * n:P * (n + 1)],
                                  wl[:, k, P * n:P * (n + 1)], hid_hi[:, step % 2, k, :], hid_lo[:, step % 2, k, :],
                                  False, last and k == 1)
                    if last and k == 1 and n in (1, 3, 5):
                        ins.then_inc(acc_done, 1)
                ins.then_inc(unit_done, 1)

            def ffn(s):
                base, f, conv = W0[s], FFN_NO[s], KINDS[s] == "conv"
                for b in range(4):
                    mm(A[b][:, :], zeros[:, 0:P], zeros[:, :], start=True, stop=False, skip_group_check=True)
                first_unit(s, G[0])
                unit(base + 1, G[1])
                if N_ADA[s]:
                    ada_reduce(s, 0)
                with pe.Fori(0, PAIRS) as i:
                    for e in range(2):
                        j = e + 1
                        u = base + 3 * j - 1
                        if conv:
                            pe.wait_ge(conv_done, at(4 * j - 2, i, 8))
                        else:
                            pe.wait_ge(mul_done, at(FIT * f + j, i, 2))
                        unit(u, G[0], i)
                        if conv:
                            pe.wait_ge(conv_done, at(4 * j, i, 8))
                        unit(u + 1, G[1], i)
                        if N_ADA[s]:
                            ada_reduce(s, j, i)
                        pe.wait_ge(hid_ready, at(FIT * f + j, i, 2))
                        down(u + 2, j - 1, "rows first", i)
                pe.wait_ge(hid_ready, FIT * (f + 1))
                down(base + 3 * FIT - 1, FIT - 1, "tiles first")

            def q_sums(s, u):
                q = QK_UNITS[KINDS[s]].index(u)
                pe.wait_ge(qsq_ready, QK0[s] + q + 1)
                if q:
                    pe.wait_ge(qstd_ready, QK0[s] + q)
                for n in range(4):
                    ins = mm(A[1][:, 2 * n:2 * n + 2], sq[:, 2 * (q % 2) + n // 2, P * (n % 2):P * (n % 2 + 1)], head_cols,
                             start=True, stop=True)
                ins.then_inc(qs_done, 1)

            def q_broadcast(s, u):
                q = QK_UNITS[KINDS[s]].index(u)
                pe.wait_ge(qrs_ready, QK0[s] + q + 1)
                if q:
                    pe.wait_ge(qc_ready, QK0[s] + q)
                for n in range(4):
                    for h in range(2):
                        ins = mm(S[HD * h:HD * (h + 1), P * n:P * (n + 1)],
                                 hstd[:, q % 2, 2 * n + h:2 * n + h + 1].to_broadcast([P, HD]), ident, start=True, stop=True)
                ins.then_inc(qb_done, 1)

            def logits(s, h):
                n = HEAD0[s] + h
                if n >= 2:
                    pe.wait_ge(am_done, n - 1)
                L, row = A[n % 2], HD * (h % 2)
                q = QT[row:row + HD, h // 2, :]
                k = (KT[row:row + HD, 4 + h // 4, :] if KINDS[s] == "swa" else KT[row:row + HD, h // 2, :])
                mm(L[:, 0:P], q[:, 0:P], k[:, 0:P], start=True, stop=True)
                mm(L[:, P:384], q[:, P:T], k, start=True, stop=True).then_inc(qk_done, 1)

            def turn(s, h):
                n = HEAD0[s] + h
                pe.wait_ge(nm_done, n + 1)
                if n:
                    pe.wait_ge(ptc_done, n)
                for c in range(3):
                    ins = nc.tensor.transpose(A[2][:, P * c:P * (c + 1)], P_of[n % 3][:, P * c:P * (c + 1)], ident)
                ins.then_inc(tr_done, 1)

            def values(s, h):
                n = HEAD0[s] + h
                pair = n // 2
                pe.wait_ge(ptc_done, n + 1)
                if h % 2 == 0 and pair >= 2:
                    pe.wait_ge(olo_done, pair - 1)
                v = h // 4 if KINDS[s] == "swa" else h
                if (KINDS[s] == "swa" and h == 0) or (KINDS[s] != "swa" and h % 4 == 0):
                    pe.wait_ge(v_ready, V0[s] + v // 4 + 1)
                row = HD * (h % 2)
                Z, pt = (A[3], S)[pair % 2], PT_of[n % 2]
                mm(Z[row:row + HD, 0:T], V[:, 0, HD * v:HD * (v + 1)], pt[:, 0:T], start=True, stop=False,
                   skip_group_check=True)
                mm(Z[row:row + HD, P:T], V[:, 1, HD * v:HD * (v + 1)], pt[:, T:384], start=False, stop=True,
                   skip_group_check=True).then_inc(pv_done, 1)

            def attention_step(s, t):
                nh = HEADS[KINDS[s]]
                if t == 0:
                    logits(s, 0)
                if t + 1 < nh:
                    logits(s, t + 1)
                if 0 <= t - 2 < nh:
                    turn(s, t - 2)
                if 0 <= t - 3 < nh:
                    values(s, t - 3)
                for _ in range(QUARTERS[KINDS[s]].count(t)):
                    direct_quarter(s, reduced[s], quarters[s] % 4)
                    quarters[s] += 1
                    if quarters[s] % 4 == 0:
                        reduced[s] += 1

            reduced = [0] * len(KINDS)
            quarters = [0] * len(KINDS)

            def reduces(s, u):
                while (reduced[s] < N_ADA[s] and ADA_AFTER[KINDS[s]][reduced[s]] <= u
                       and (reduced[s] not in DIRECT[KINDS[s]] or u > 20)):
                    ada_reduce(s, reduced[s])
                    reduced[s] += 1

            def q_unit(s, u):
                kind = KINDS[s]
                qk = QK_UNITS[kind]
                reduces(s, u)
                if u - 4 in qk:
                    pe.wait_ge(qk_ready, QK0[s] + qk.index(u - 4) + 1)
                if kind == "swa" and u == 5:
                    pe.wait_ge(v_ready, V0[s] + 1)
                do = v_half if u in V_UNITS[kind] else half
                do(W0[s] + u, bank_of(s, u), 0)
                if u - 2 in qk:
                    q_broadcast(s, u - 2)
                if u - 1 in qk:
                    q_sums(s, u - 1)
                do(W0[s] + u, bank_of(s, u), 1)

            def out_units(s, xh, xl):
                kind = KINDS[s]
                for o in range(4):
                    u = OUT_UNITS[kind] + o
                    reduces(s, u)
                    if o >= 2:
                        pe.wait_ge(x_ready, KD * (s + 1) + 2 * (o - 1))
                    half(W0[s] + u, G[o % 2], 0, xh, xl)
                    half(W0[s] + u, G[o % 2], 1, xh, xl)
                reduces(s, NUNITS[kind] + 1)

            def direct(n):
                r = PRO_PE[n]
                pe.wait_ge(raw_full[n], 16)
                times_c(raw[:, n, :].rearrange("p (k n) -> p k n", k=KD), 2 * r, 0).then_inc(pro_done, 1)

            def pro_reduce(n):
                sum_partitions(n, 2 * PRO_DVE[n])

            pe.wait_ge(c_full, 48)
            nc.tensor.transpose(S[:, 0:16], c_rows[:, :], ident[0:16, 0:16]).then_inc(c_turned, 1)
            pe.wait_ge(c_done, 1)
            direct(0)
            pe.wait_ge(x_full, 16)
            for k in range(KD):
                for t in range(2):
                    ins = nc.tensor.transpose(A[k // 2][:, T * (k % 2) + P * t:T * (k % 2) + P * (t + 1)],
                                              x_in[:, t, P * k:P * (k + 1)], ident)
                if k % 2:
                    ins.then_inc(x_turned, 1)
            pe.wait_ge(rows_full, ROWS_LOADED)
            for t in range(4):
                ins = nc.tensor.transpose(G[0][:, P * t:P * (t + 1)], rows[:, t, :], ident)
            ins.then_inc(rows_turned, 1)
            pro_reduce(0)
            pe.wait_ge(small_full, SMALL_LOADED)
            pe.wait_ge(ones_set, 1)
            pe.wait_ge(cols_done, 2)
            for n in range(2):
                heads = (8, 16)[n]
                mm(G[n][0:heads, 0:384], rel[0:33, 8 * n:8 * n + heads], tables[:, 384 * n:384 * (n + 1)],
                   start=True, stop=True).then_inc(bias_sum, 1)
            norm(0)
            pro_reduce(1)
            direct(1)
            for n in range(2, len(PRO_DVE)):
                pro_reduce(n)

            for s, kind in enumerate(KINDS):
                base = W0[s]
                if s:
                    norm(s)
                if kind in ("conv", "ffn"):
                    ffn(s)
                    if N_ADA[s]:
                        ada_reduce(s, 11)
                elif kind == "moba":
                    first_unit(s, G[0])
                    for u in range(1, 5):
                        q_unit(s, u)
                    q_broadcast(s, 3)
                    for t in range(HEADS[kind] + 3):
                        if t == 0:
                            pe.wait_ge(qk_ready, QK0[s] + 4)
                        attention_step(s, t)
                        if t < 6:
                            u = 5 + t // 2
                            if t % 2 == 0:
                                reduces(s, u)
                            if u == 5:
                                v_half(base + u, G[u % 2], t % 2)
                            else:
                                if t == 2:
                                    pe.wait_ge(v_ready, V0[s] + 1)
                                if t == 4:
                                    pe.wait_ge(v_ready, V0[s] + 2)
                                half(base + u, G[u % 2], t % 2)
                    for r in range(8):
                        reduces(s, 8 + r)
                        if r < 2:
                            pe.wait_ge(p_ready, r + 1)
                        else:
                            pe.wait_ge(sig_ready, r - 1)
                        half(base + 8 + r, G[r % 2], 0)
                        half(base + 8 + r, G[r % 2], 1)
                        if r == 5:
                            pe.wait_ge(pool_ready, 4)
                            for g in range(4):
                                mm(A[g // 2][:, T * (g % 2):T * (g % 2 + 1)], pool_w[:, g, :],
                                   std[:, g // 2, T * (g % 2):T * (g % 2 + 1)], start=True, stop=True).then_inc(pw_done, 1)
                    pe.wait_ge(pool_split, 1)
                    for m in range(4):
                        u = 16 + m
                        reduces(s, u)
                        if m >= 2:
                            pe.wait_ge((merge_a, merge_b)[m % 2], 2)
                        pe.wait_ge(lo_ready, base + u + 1)
                        wh, wl = unit_of(base + u, 4)
                        x0 = 4 * (m % 2)
                        for n in range(4):
                            for k in range(4):
                                ins = product(A[2 * (m % 2) + n // 2][:, T * (n % 2):T * (n % 2 + 1)],
                                              wh[:, k, P * n:P * (n + 1)], wl[:, k, P * n:P * (n + 1)],
                                              o_hi[:, x0 + k, :], o_lo[:, x0 + k, :], k == 0, k == 3)
                        ins.then_inc(unit_done, 1)
                    reduces(s, 21)
                    pe.wait_ge(merged, 4)
                    out_units(s, h_hi, h_lo)
                elif kind == "swa":
                    first_unit(s, G[0])
                    for u in range(1, 6):
                        if u == 5:
                            pe.wait_ge(qk_ready, QK0[s] + 2)
                            for g in range(4):
                                dup = kon[:, K_DUP + P * (g % 2):K_DUP + P * (g % 2 + 1)]
                                ins = mm(A[g // 2 * 2][:, T * (g % 2):T * (g % 2 + 1)], dup, KT[:, g // 2, :], start=True, stop=True)
                                if g % 2:
                                    ins.then_inc(dup_done, 1)
                        q_unit(s, u)
                    q_broadcast(s, 4)
                    q_sums(s, 5)
                    q_broadcast(s, 5)
                    pe.wait_ge(dup_ready, 2)
                    pe.wait_ge(qk_ready, QK0[s] + 5)
                    for t in range(HEADS[kind] + 3):
                        attention_step(s, t)
                    pe.wait_ge(olo_done, (HEAD0[s] + HEADS[kind]) // 2)
                    out_units(s, o_hi, o_lo)
                else:
                    first_unit(s, G[0])
                    pe.wait_ge(f_lo_done, 1)
                    for t in range(2):
                        for k in range(KD):
                            ins = product(A[0][:, 16 * t:16 * (t + 1)], h_hi[:, k, P * t:P * (t + 1)],
                                          h_lo[:, k, P * t:P * (t + 1)], f_hi[:, k, :], f_lo[:, k, :], k == 0, k == KD - 1)
                    ins.then_inc(fl_done, 1)
                    for u in range(1, 9):
                        if u == 4:
                            pe.wait_ge(lf_ready, 1)
                            lf = fz[:, 4, :]
                            mm(A[0][:, 64:80], tri, lf[:, 0:16], start=True, stop=True)
                            mm(A[0][:, 80:96], ones[:, :], lf[:, 0:16], start=True, stop=False)
                            mm(A[0][:, 80:96], tri, lf[:, 16:32], start=False, stop=True).then_inc(cum_done, 1)
                        if u == 6:
                            pe.wait_ge(fq_ready, 1)
                            for t in range(2):
                                ins = nc.tensor.transpose(A[0][0:16, P * (t + 1):P * (t + 2)], Fq[:, t, :], ident)
                            ins.then_inc(ft_done, 1)
                        q_unit(s, u)
                    q_broadcast(s, 7)
                    pe.wait_ge(qk_ready, QK0[s] + 8)
                    for t in range(HEADS[kind] + 3):
                        attention_step(s, t)
                        if t in (1, 2, 5, 6, 9, 10):
                            u = 9 + t // 4
                            n = (t - 1) % 4
                            if n == 0:
                                reduces(s, u)
                                if u > 9:
                                    pe.wait_ge(v_ready, V0[s] + u - 9)
                            v_half(base + u, G[u % 2], n)
                    pe.wait_ge(olo_done, (HEAD0[s] + HEADS[kind]) // 2)
                    out_units(s, o_hi, o_lo)
            for b in range(4):
                pe.wait_ge(x_ready, KD * len(KINDS) + 4 * (b % 2) + 4)
                for k in range(4):
                    ins = nc.tensor.transpose((G[0], G[1], M, S)[b][:, P * k:P * (k + 1)],
                                              xT[:, 4 * (b % 2) + k, P * (b // 2):P * (b // 2 + 1)], ident)
                ins.then_inc(y_turned, 1)


def constants():
    k = np.zeros((P, K_END), np.float32)
    i, j = np.arange(P)[:, None], np.arange(P)[None, :]
    k[:, K_IDENT:K_IDENT + P] = i == j
    k[:, K_HEADS:K_HEADS + 2] = i // HD == np.arange(2)[None, :]
    k[:, K_TRI:K_TRI + P] = i <= j
    k[:, K_MASK + P:K_MASK + 2 * P] = np.where(j <= i, 0.0, NEG)
    for h in range(2):
        k[:, K_DUP + P * h:K_DUP + P * (h + 1)] = i == j % HD + HD * h
    for g, w in enumerate(WINDOWS):
        k[:, K_INV + 16 * g:K_INV + 16 * (g + 1)] = 1.0 / np.minimum(np.arange(16) + 1, w)
    return k


def bucket_tables():
    t = np.zeros((33, 2, 384), np.float32)
    for n, window in enumerate((T, P)):
        for x in range(384):
            d = T - 1 - x
            if not 0 <= d < window:
                t[32, n, x] = NEG
            elif d < 16:
                t[d, n, x] = 1.0
            else:
                t[min(16 + int(np.log(d / 16) / np.log(128 / 16) * 16), 31), n, x] = 1.0
    return t.reshape(33, 768)


def kernel(**inputs):
    import concourse.bacc as bacc
    from concourse.bass_utils import run_bass_kernel_spmd

    nc = bacc.Bacc("TRN2", target_bir_lowering=False, num_devices=1)
    arrays, aps = {}, {}
    for name, value in {**inputs, "constants": constants(), "bucket_tables": bucket_tables()}.items():
        value = np.ascontiguousarray(value)
        arrays[f"in_{name}"] = value
        aps[name] = nc.dram_tensor(f"in_{name}", value.shape, mybir.dt.from_np(value.dtype), kind="ExternalInput").ap()
    out = nc.dram_tensor("out", (1, T, D), F32, kind="ExternalOutput").ap()
    build(nc, aps, aps["constants"], aps["bucket_tables"], out)
    r = run_bass_kernel_spmd(nc, [arrays], core_ids=[0])
    return r.results[0]["out"]
```
